# Optimizing a Trainium2 kernel written in Bass

```python
import jax, jax.numpy as jnp
from jax import lax
import numpy as np
import math

D_MODEL = 1024
BATCH = 1
SEQ = 256
DEPTH = 1

CHUNK = 64
PLE_DIM = 256
EPS = 1e-6

D_SGU = 1024
SGU_BLOCK = 128
SGU_HEADS = 8
SGU_HEAD_DIM = D_SGU // SGU_HEADS

D_CONV = 1024
CONV_WIDTH = 31

D_POOL = 1024
POOL_WINDOWS = (2, 4, 8, 16)
POOL_GROUPS = len(POOL_WINDOWS)
POOL_GROUP_DIM = D_POOL // POOL_GROUPS

N_BRANCH = 3
D_IN = 2 * D_SGU + 2 * D_CONV + D_POOL + N_BRANCH * D_MODEL
SPLITS = (2 * D_SGU, 2 * D_SGU + 2 * D_CONV, 2 * D_SGU + 2 * D_CONV + D_POOL)

D_FF = -(-8 * D_MODEL // (3 * 256)) * 256


def rms_norm(x, g):
    xf = x.astype(jnp.float32)
    y = xf * lax.rsqrt(jnp.mean(xf * xf, axis=-1, keepdims=True) + EPS)
    return (y * g.astype(jnp.float32)).astype(x.dtype)

def layer_norm(x, g, b):
    xf = x.astype(jnp.float32)
    mu = jnp.mean(xf, axis=-1, keepdims=True)
    xc = xf - mu
    var = jnp.mean(xc * xc, axis=-1, keepdims=True)
    y = xc * lax.rsqrt(var + EPS) * g.astype(jnp.float32) + b.astype(jnp.float32)
    return y.astype(x.dtype)

def sgu_mask():
    c = jnp.arange(SGU_BLOCK) // CHUNK
    return c[None, :] <= c[:, None]

def spatial_gating(z, w_s, b_s, g_v, b_v):
    u, v = jnp.split(z, 2, axis=-1)
    v = layer_norm(v, g_v, b_v)
    bsz, s, _ = v.shape
    nb = s // SGU_BLOCK
    v = v.reshape(bsz, nb, SGU_BLOCK, SGU_HEADS, SGU_HEAD_DIM)
    w = jnp.where(sgu_mask()[None], w_s, jnp.zeros_like(w_s))
    mixed = jnp.einsum('hij,bnjhc->bnihc', w, v) + b_s.T[None, None, :, :, None]
    return u * mixed.reshape(bsz, s, D_SGU)

def conformer_conv(z, w_dw, b_dw, g_ln, b_ln):
    a, gate = jnp.split(z, 2, axis=-1)
    h = a * jax.nn.sigmoid(gate)
    h = lax.conv_general_dilated(
        h, w_dw, window_strides=(1,), padding=((CONV_WIDTH - 1, 0),),
        dimension_numbers=('NWC', 'WIO', 'NWC'),
        feature_group_count=D_CONV) + b_dw
    h = layer_norm(h, g_ln, b_ln)
    return jax.nn.silu(h)

def multiscale_pool(z, w_pool, s_pool):
    bsz, s, _ = z.shape
    zf = z.astype(jnp.float32)
    cs = jnp.cumsum(zf, axis=1)
    t = jnp.arange(1, s + 1, dtype=jnp.float32)
    outs = []
    for gi, w in enumerate(POOL_WINDOWS):
        sl = slice(gi * POOL_GROUP_DIM, (gi + 1) * POOL_GROUP_DIM)
        c = cs[..., sl]
        prev = jnp.pad(c[:, :s - w], ((0, 0), (w, 0), (0, 0)))
        cnt = jnp.minimum(t, float(w))[None, :, None]
        outs.append((c - prev) / cnt - zf[..., sl])
    pooled = jnp.stack(outs, axis=2).astype(z.dtype)
    mixed = jnp.einsum('bsgc,gcd->bsgd', pooled, w_pool)
    return mixed.reshape(bsz, s, D_POOL) * s_pool

def first_inputs(seed: int = 0) -> dict:
    key = jax.random.key(seed)
    ks = jax.random.split(key, 32)
    f32 = jnp.float32

    def nrm(k, shape, scale):
        return jax.random.normal(k, shape, f32) * scale

    def gain(k, shape):
        return 1.0 + 0.05 * jax.random.normal(k, shape, f32)

    L = DEPTH
    return {
        "x": nrm(ks[0], (BATCH, SEQ, D_MODEL), 1.0),
        "p": nrm(ks[1], (DEPTH, BATCH, SEQ, PLE_DIM), 1.0),
        "g_mix_pre": gain(ks[2], (L, D_MODEL)),
        "w_in": nrm(ks[3], (L, D_MODEL, D_IN), D_MODEL ** -0.5),
        "w_sgu_s": nrm(ks[4], (L, SGU_HEADS, SGU_BLOCK, SGU_BLOCK), SGU_BLOCK ** -0.5),
        "b_sgu_s": 1.0 + 0.1 * jax.random.normal(ks[5], (L, SGU_HEADS, SGU_BLOCK), f32),
        "g_sgu_v": gain(ks[6], (L, D_SGU)),
        "b_sgu_v": nrm(ks[7], (L, D_SGU), 0.02),
        "w_sgu_out": nrm(ks[8], (L, D_SGU, D_MODEL), D_SGU ** -0.5),
        "w_dw": nrm(ks[9], (L, CONV_WIDTH, 1, D_CONV), CONV_WIDTH ** -0.5),
        "b_dw": nrm(ks[10], (L, D_CONV), 0.02),
        "g_conv_ln": gain(ks[11], (L, D_CONV)),
        "b_conv_ln": nrm(ks[12], (L, D_CONV), 0.02),
        "w_conv_out": nrm(ks[13], (L, D_CONV, D_MODEL), D_CONV ** -0.5),
        "w_pool": nrm(ks[14], (L, POOL_GROUPS, POOL_GROUP_DIM, POOL_GROUP_DIM), POOL_GROUP_DIM ** -0.5),
        "s_pool": 1.0 + 0.1 * jax.random.normal(ks[15], (L, D_POOL), f32),
        "w_pool_out": nrm(ks[16], (L, D_POOL, D_MODEL), D_POOL ** -0.5),
        "w_out": nrm(ks[17], (L, D_MODEL, D_MODEL), D_MODEL ** -0.5),
        "g_mix_post": gain(ks[18], (L, D_MODEL)),
        "g_ffn_pre": gain(ks[19], (L, D_MODEL)),
        "w_ffn_in": nrm(ks[20], (L, D_MODEL, 2 * D_FF), D_MODEL ** -0.5),
        "w_ffn_out": nrm(ks[21], (L, D_FF, D_MODEL), D_FF ** -0.5),
        "g_ffn_post": gain(ks[22], (L, D_MODEL)),
        "w_ple": nrm(ks[23], (L, PLE_DIM, D_MODEL), PLE_DIM ** -0.5),
        "w_ple_gate": nrm(ks[24], (L, D_MODEL, D_MODEL), D_MODEL ** -0.5),
    }

def first_block(x, p, g_mix_pre, w_in, w_sgu_s, b_sgu_s, g_sgu_v, b_sgu_v, w_sgu_out,
              w_dw, b_dw, g_conv_ln, b_conv_ln, w_conv_out, w_pool, s_pool, w_pool_out,
              w_out, g_mix_post, g_ffn_pre, w_ffn_in, w_ffn_out, g_ffn_post,
              w_ple, w_ple_gate):
    h = x
    bsz, s, _ = x.shape
    for i in range(DEPTH):
        hn = rms_norm(h, g_mix_pre[i])
        proj = hn @ w_in[i]
        z_sgu, z_conv, z_pool, z_gate = jnp.split(proj, SPLITS, axis=-1)

        br_a = spatial_gating(jax.nn.gelu(z_sgu), w_sgu_s[i], b_sgu_s[i],
                              g_sgu_v[i], b_sgu_v[i]) @ w_sgu_out[i]
        br_b = conformer_conv(z_conv, w_dw[i], b_dw[i],
                              g_conv_ln[i], b_conv_ln[i]) @ w_conv_out[i]
        br_c = multiscale_pool(z_pool, w_pool[i], s_pool[i]) @ w_pool_out[i]

        gates = jax.nn.sigmoid(z_gate).reshape(bsz, s, N_BRANCH, D_MODEL)
        merged = gates[:, :, 0] * br_a + gates[:, :, 1] * br_b + gates[:, :, 2] * br_c
        h = h + rms_norm(merged @ w_out[i], g_mix_post[i])

        hn = rms_norm(h, g_ffn_pre[i])
        f_gate, f_up = jnp.split(hn @ w_ffn_in[i], 2, axis=-1)
        f = (jax.nn.silu(f_gate) * f_up) @ w_ffn_out[i]
        h = h + rms_norm(f, g_ffn_post[i])

        h = h + jax.nn.sigmoid(h @ w_ple_gate[i]) * (p[i] @ w_ple[i])
    return h


DEPTH_2 = 2

N_MIXERS = 2
N_RET_LAYERS = (DEPTH_2 + 1) // 2
N_MLA_LAYERS = DEPTH_2 // 2
DN_ALPHA = (2.0 * DEPTH_2) ** 0.25
DN_BETA = (8.0 * DEPTH_2) ** -0.25
LN_EPS = 1e-5
ROPE_BASE = 10000.0

RET_HEADS = 4
RET_DK = D_MODEL // RET_HEADS
RET_DV = 2 * RET_DK
RET_HK = RET_HEADS * RET_DK
RET_HV = RET_HEADS * RET_DV
RET_IN = 2 * RET_HK + 2 * RET_HV
RET_CHUNK = 128

MLA_HEADS = 8
MLA_NOPE = 128
MLA_ROPE = 64
MLA_VDIM = 128
MLA_Q_RANK = 384
MLA_KV_RANK = 256
MLA_IN = MLA_Q_RANK + MLA_KV_RANK + MLA_ROPE
MLA_QBLOCK = 128

PEER_HEADS = 8
PEER_NKEYS = 128
PEER_EXPERTS = PEER_NKEYS * PEER_NKEYS
PEER_DKEY = 256
PEER_HALF = PEER_DKEY // 2
PEER_TOPK = 16
PEER_TOKEN_BLOCK = 128


def layer_norm_2(x, g, b):
    xf = x.astype(jnp.float32)
    mu = jnp.mean(xf, axis=-1, keepdims=True)
    var = jnp.mean(jnp.square(xf - mu), axis=-1, keepdims=True)
    return ((xf - mu) * lax.rsqrt(var + LN_EPS) * g.astype(jnp.float32) + b.astype(jnp.float32)).astype(x.dtype)

def rms_norm_2(x, g):
    xf = x.astype(jnp.float32)
    ms = jnp.mean(jnp.square(xf), axis=-1, keepdims=True)
    return (xf * lax.rsqrt(ms + LN_EPS) * g.astype(jnp.float32)).astype(x.dtype)

def rotary(x, positions):
    d = x.shape[-1]
    inv_freq = ROPE_BASE ** (-jnp.arange(0, d, 2, dtype=jnp.float32) / d)
    ang = positions.astype(jnp.float32)[..., None] * inv_freq
    cos = jnp.cos(ang)[:, :, None, :]
    sin = jnp.sin(ang)[:, :, None, :]
    x1, x2 = jnp.split(x.astype(jnp.float32), 2, axis=-1)
    return jnp.concatenate([x1 * cos - x2 * sin, x1 * sin + x2 * cos], axis=-1).astype(x.dtype)

def retention_scan(q, k, v, log_gamma, strict):
    B, S, H, dk = q.shape
    dv = v.shape[-1]
    C = RET_CHUNK
    n_chunks = S // C
    dt = q.dtype
    idx = jnp.arange(C, dtype=jnp.float32)
    diff = idx[:, None] - idx[None, :]
    keep = (diff > 0) if strict else (diff >= 0)
    lg = log_gamma[:, None, None]
    decay = jnp.where(keep[None], jnp.exp(jnp.maximum(diff, 0.0)[None] * lg), 0.0).astype(dt)
    xi = jnp.exp((idx + 1.0)[None, :] * log_gamma[:, None]).astype(dt)
    zeta = jnp.exp((C - 1.0 - idx)[None, :] * log_gamma[:, None]).astype(dt)
    gamma_c = jnp.exp(C * log_gamma).astype(dt)[None, :, None, None]

    def to_chunks(t):
        return t.reshape(B, n_chunks, C, H, t.shape[-1]).transpose(1, 0, 3, 2, 4)

    def step(state, inp):
        qi, ki, vi = inp
        inner = jnp.einsum('bhnm,bhmv->bhnv', jnp.einsum('bhnd,bhmd->bhnm', qi, ki) * decay[None], vi)
        cross = jnp.einsum('bhnd,bhdv->bhnv', qi, state) * xi[None, :, :, None]
        state = gamma_c * state + jnp.einsum('bhmd,bhmv->bhdv', ki * zeta[None, :, :, None], vi)
        return state, inner + cross

    state0 = jnp.zeros((B, H, dk, dv), dt)
    _, out = lax.scan(step, state0, (to_chunks(q), to_chunks(k), to_chunks(v)))
    return out.transpose(1, 0, 3, 2, 4).reshape(B, S, H, dv)

def retention_mixer(x, positions, w_in, log1m_decay, gn_g, gn_b, w_out):
    B, S, _ = x.shape
    proj = x @ w_in
    q, k, v, g = jnp.split(proj, [RET_HK, 2 * RET_HK, 2 * RET_HK + RET_HV], axis=-1)
    q = rotary(q.reshape(B, S, RET_HEADS, RET_DK), positions)
    k = rotary(k.reshape(B, S, RET_HEADS, RET_DK), positions) * (RET_DK ** -0.5)
    v = v.reshape(B, S, RET_HEADS, RET_DV)
    log_gamma = jnp.log1p(-jnp.exp(log1m_decay.astype(jnp.float32)))
    fwd = retention_scan(q, k, v, log_gamma[0], strict=False)
    bwd = jnp.flip(retention_scan(jnp.flip(q, 1), jnp.flip(k, 1), jnp.flip(v, 1), log_gamma[1], strict=True), 1)
    y = (fwd + bwd).astype(jnp.float32)
    mu = jnp.mean(y, axis=-1, keepdims=True)
    var = jnp.mean(jnp.square(y - mu), axis=-1, keepdims=True)
    yn = ((y - mu) * lax.rsqrt(var + LN_EPS)).reshape(B, S, RET_HV)
    yn = (yn * gn_g.astype(jnp.float32) + gn_b.astype(jnp.float32)).astype(x.dtype)
    return (jax.nn.silu(g) * yn) @ w_out

def mla_mixer(x, positions, w_in, q_norm_g, kv_norm_g, w_uq, w_ukv, w_out):
    B, S, _ = x.shape
    c_q, c_kv, k_rope = jnp.split(x @ w_in, [MLA_Q_RANK, MLA_Q_RANK + MLA_KV_RANK], axis=-1)
    q = (rms_norm_2(c_q, q_norm_g) @ w_uq).reshape(B, S, MLA_HEADS, MLA_NOPE + MLA_ROPE)
    q_nope, q_rope = jnp.split(q, [MLA_NOPE], axis=-1)
    q_rope = rotary(q_rope, positions)
    kv = (rms_norm_2(c_kv, kv_norm_g) @ w_ukv).reshape(B, S, MLA_HEADS, MLA_NOPE + MLA_VDIM)
    k_nope, v = jnp.split(kv, [MLA_NOPE], axis=-1)
    k_rope = rotary(k_rope[:, :, None, :], positions)[:, :, 0, :]
    scale = (MLA_NOPE + MLA_ROPE) ** -0.5
    nb = S // MLA_QBLOCK

    def blocks(t):
        return t.reshape(B, nb, MLA_QBLOCK, MLA_HEADS, t.shape[-1]).transpose(1, 0, 2, 3, 4)

    def attend(blk):
        qn, qr = blk
        s = jnp.einsum('bqhd,bkhd->bhqk', qn, k_nope) + jnp.einsum('bqhd,bkd->bhqk', qr, k_rope)
        p = jax.nn.softmax(s.astype(jnp.float32) * scale, axis=-1).astype(v.dtype)
        return jnp.einsum('bhqk,bkhd->bqhd', p, v)

    o = lax.map(attend, (blocks(q_nope), blocks(q_rope)))
    o = o.transpose(1, 0, 2, 3, 4).reshape(B, S, MLA_HEADS * MLA_VDIM)
    return o @ w_out

def peer_ffn(x, w_q, sub_keys, u, v):
    B, S, D = x.shape
    T = B * S
    xt = x.reshape(T // PEER_TOKEN_BLOCK, PEER_TOKEN_BLOCK, D)

    def block(xb):
        q = (xb @ w_q).reshape(PEER_TOKEN_BLOCK, PEER_HEADS, 2, PEER_HALF)
        s = jnp.einsum('thcd,hckd->thck', q, sub_keys).astype(jnp.float32)
        s1, i1 = lax.top_k(s[:, :, 0], PEER_TOPK)
        s2, i2 = lax.top_k(s[:, :, 1], PEER_TOPK)
        cand_s = (s1[..., :, None] + s2[..., None, :]).reshape(PEER_TOKEN_BLOCK, PEER_HEADS, PEER_TOPK * PEER_TOPK)
        cand_i = (i1[..., :, None] * PEER_NKEYS + i2[..., None, :]).reshape(PEER_TOKEN_BLOCK, PEER_HEADS, PEER_TOPK * PEER_TOPK)
        top_s, pos = lax.top_k(cand_s, PEER_TOPK)
        eidx = jnp.take_along_axis(cand_i, pos, axis=-1)
        gate = jax.nn.softmax(top_s, axis=-1).astype(xb.dtype)
        h = jax.nn.gelu(jnp.einsum('thkd,td->thk', u[eidx], xb), approximate=False)
        return jnp.einsum('thk,thkd->td', gate * h, v[eidx])

    return lax.map(block, xt).reshape(B, S, D)

def second_inputs(seed: int = 0) -> dict:
    key = jax.random.key(seed)
    ks = jax.random.split(key, 24)
    f32 = jnp.float32
    nrm = lambda k, shape, s: jax.random.normal(k, shape, f32) * s
    x = jax.random.normal(ks[0], (BATCH, SEQ, D_MODEL), f32)
    offsets = jax.random.randint(ks[1], (BATCH, 1), 0, 512, dtype=jnp.int32)
    positions = (offsets + jnp.arange(SEQ, dtype=jnp.int32)[None, :]).astype(jnp.int32)
    ret_w_in = nrm(ks[2], (N_RET_LAYERS, D_MODEL, RET_IN), D_MODEL ** -0.5)
    base = (-5.0 - jnp.arange(RET_HEADS, dtype=f32)) * math.log(2.0)
    ret_log1m_decay = base[None, None, :] + nrm(ks[3], (N_RET_LAYERS, 2, RET_HEADS), 0.05)
    ret_gn_g = 1.0 + nrm(ks[4], (N_RET_LAYERS, RET_HV), 0.02)
    ret_gn_b = nrm(ks[5], (N_RET_LAYERS, RET_HV), 0.02)
    ret_w_out = nrm(ks[6], (N_RET_LAYERS, RET_HV, D_MODEL), DN_BETA * RET_HV ** -0.5)
    mla_w_in = nrm(ks[7], (N_MLA_LAYERS, D_MODEL, MLA_IN), D_MODEL ** -0.5)
    mla_q_norm = 1.0 + nrm(ks[8], (N_MLA_LAYERS, MLA_Q_RANK), 0.02)
    mla_kv_norm = 1.0 + nrm(ks[9], (N_MLA_LAYERS, MLA_KV_RANK), 0.02)
    mla_w_uq = nrm(ks[10], (N_MLA_LAYERS, MLA_Q_RANK, MLA_HEADS * (MLA_NOPE + MLA_ROPE)), MLA_Q_RANK ** -0.5)
    mla_w_ukv = nrm(ks[11], (N_MLA_LAYERS, MLA_KV_RANK, MLA_HEADS * (MLA_NOPE + MLA_VDIM)), MLA_KV_RANK ** -0.5)
    mla_w_out = nrm(ks[12], (N_MLA_LAYERS, MLA_HEADS * MLA_VDIM, D_MODEL), DN_BETA * (MLA_HEADS * MLA_VDIM) ** -0.5)
    peer_w_q = nrm(ks[13], (DEPTH_2, D_MODEL, PEER_HEADS * PEER_DKEY), D_MODEL ** -0.5)
    peer_sub_keys = nrm(ks[14], (DEPTH_2, PEER_HEADS, 2, PEER_NKEYS, PEER_HALF), PEER_HALF ** -0.5)
    peer_u = nrm(ks[15], (DEPTH_2, PEER_EXPERTS, D_MODEL), D_MODEL ** -0.5)
    peer_v = nrm(ks[16], (DEPTH_2, PEER_EXPERTS, D_MODEL), DN_BETA * (PEER_HEADS * PEER_TOPK) ** -0.5)
    ln_mix_g = 1.0 + nrm(ks[17], (DEPTH_2, D_MODEL), 0.02)
    ln_mix_b = nrm(ks[18], (DEPTH_2, D_MODEL), 0.02)
    ln_ffn_g = 1.0 + nrm(ks[19], (DEPTH_2, D_MODEL), 0.02)
    ln_ffn_b = nrm(ks[20], (DEPTH_2, D_MODEL), 0.02)
    return {'x': x, 'positions': positions,
            'ret_w_in': ret_w_in, 'ret_log1m_decay': ret_log1m_decay, 'ret_gn_g': ret_gn_g, 'ret_gn_b': ret_gn_b, 'ret_w_out': ret_w_out,
            'mla_w_in': mla_w_in, 'mla_q_norm': mla_q_norm, 'mla_kv_norm': mla_kv_norm, 'mla_w_uq': mla_w_uq, 'mla_w_ukv': mla_w_ukv, 'mla_w_out': mla_w_out,
            'peer_w_q': peer_w_q, 'peer_sub_keys': peer_sub_keys, 'peer_u': peer_u, 'peer_v': peer_v,
            'ln_mix_g': ln_mix_g, 'ln_mix_b': ln_mix_b, 'ln_ffn_g': ln_ffn_g, 'ln_ffn_b': ln_ffn_b}

def second_block(x, positions,
              ret_w_in, ret_log1m_decay, ret_gn_g, ret_gn_b, ret_w_out,
              mla_w_in, mla_q_norm, mla_kv_norm, mla_w_uq, mla_w_ukv, mla_w_out,
              peer_w_q, peer_sub_keys, peer_u, peer_v,
              ln_mix_g, ln_mix_b, ln_ffn_g, ln_ffn_b):
    h = x
    for i in range(DEPTH_2):
        j = i // N_MIXERS
        if i % N_MIXERS == 0:
            mix = retention_mixer(h, positions, ret_w_in[j], ret_log1m_decay[j], ret_gn_g[j], ret_gn_b[j], ret_w_out[j])
        else:
            mix = mla_mixer(h, positions, mla_w_in[j], mla_q_norm[j], mla_kv_norm[j], mla_w_uq[j], mla_w_ukv[j], mla_w_out[j])
        h = layer_norm_2(DN_ALPHA * h + mix, ln_mix_g[i], ln_mix_b[i])
        ffn = peer_ffn(h, peer_w_q[i], peer_sub_keys[i], peer_u[i], peer_v[i])
        h = layer_norm_2(DN_ALPHA * h + ffn, ln_ffn_g[i], ln_ffn_b[i])
    return h


def setup_inputs(seed=0):
    out = dict(first_inputs(seed))
    for name, value in second_inputs(seed + 1).items():
        if name != "x":
            out[name + "_2"] = value
    return out


def reference(
    x, p, g_mix_pre, w_in, w_sgu_s, b_sgu_s, g_sgu_v, b_sgu_v, w_sgu_out, w_dw, b_dw, g_conv_ln,
    b_conv_ln, w_conv_out, w_pool, s_pool, w_pool_out, w_out, g_mix_post, g_ffn_pre, w_ffn_in,
    w_ffn_out, g_ffn_post, w_ple, w_ple_gate, positions_2, ret_w_in_2, ret_log1m_decay_2,
    ret_gn_g_2, ret_gn_b_2, ret_w_out_2, mla_w_in_2, mla_q_norm_2, mla_kv_norm_2, mla_w_uq_2,
    mla_w_ukv_2, mla_w_out_2, peer_w_q_2, peer_sub_keys_2, peer_u_2, peer_v_2, ln_mix_g_2,
    ln_mix_b_2, ln_ffn_g_2, ln_ffn_b_2,
):
    x = first_block(
        x, p, g_mix_pre, w_in, w_sgu_s, b_sgu_s, g_sgu_v, b_sgu_v, w_sgu_out, w_dw, b_dw,
        g_conv_ln, b_conv_ln, w_conv_out, w_pool, s_pool, w_pool_out, w_out, g_mix_post,
        g_ffn_pre, w_ffn_in, w_ffn_out, g_ffn_post, w_ple, w_ple_gate,
    )
    return second_block(
        x, positions_2, ret_w_in_2, ret_log1m_decay_2, ret_gn_g_2, ret_gn_b_2, ret_w_out_2,
        mla_w_in_2, mla_q_norm_2, mla_kv_norm_2, mla_w_uq_2, mla_w_ukv_2, mla_w_out_2,
        peer_w_q_2, peer_sub_keys_2, peer_u_2, peer_v_2, ln_mix_g_2, ln_mix_b_2, ln_ffn_g_2,
        ln_ffn_b_2,
    )


_drawn_inputs = setup_inputs


def setup_inputs(seed=0):
    import zlib

    import numpy as np

    out = dict(_drawn_inputs(seed))
    spreads = {}
    factors = {'g_sgu_v': 3.093,
     'b_sgu_v': 7.964,
     'b_dw': 3.241,
     'b_conv_ln': 7.104,
     'ret_gn_g_2': 8.0,
     'ret_gn_b_2': 8.0,
     'mla_q_norm_2': 8.0,
     'mla_kv_norm_2': 8.0,
     'peer_u_2': 2.939}
    for name, (base, spread) in spreads.items():
        noise = np.random.default_rng([zlib.crc32(name.encode()), seed]).standard_normal(out[name].shape)
        drawn = base * np.exp(spread * noise) if base else spread * noise
        out[name] = __import__('jax').numpy.asarray(drawn.astype(out[name].dtype))
    for name, factor in factors.items():
        out[name] = (out[name] * factor).astype(out[name].dtype)
    return out
```

```python
import math
from contextlib import ExitStack, contextmanager

import concourse.bass as bass
from concourse import mybir

FP32 = mybir.dt.float32
I32 = mybir.dt.int32
U32 = mybir.dt.uint32
ALU = mybir.AluOpType
ACT = mybir.ActivationFunctionType
AX = mybir.AxisListType

P = 128
D = 1024
S = 256
KT = D // P
TT = S // P
EPS = 1e-6
LN_EPS = 1e-5
CONV = 31
PAD = CONV - 1
ZPAD = 16
WINDOWS = (2, 4, 8, 16)
D_FF = 2816
FT = D_FF // P
ALPHA = 4.0 ** 0.25
RET_HEADS, RET_DK, RET_DV = 4, 256, 512
MLA_HEADS = 8
MLA_SCALE = (128 + 64) ** -0.5
HEADS, TOPK, NKEYS = 8, 16, 128
EXPERTS = NKEYS * NKEYS
LOWEST = -3.0e38
TWO_PI = 2.0 * math.pi
PI_A = 6.28125
PI_B = 0.0019350051879882812
PI_C = TWO_PI - PI_A - PI_B
ROUND = 1.5 * 2.0 ** 23

TILES = 16
SLOTS = 4
BANKS = 4

STREAM = [("conv", 8), ("pool", 4), ("u", 4), ("v", 4), ("gates", 12), ("w_pool", 1), ("br_conv", 4),
          ("br_pool", 4), ("br_sgu", 4), ("w_out", 4), ("ffn_in", 22), ("ffn_out", 11), ("ple", 1),
          ("ple_gate", 4), ("ret_qk", 8), ("ret_v", 8), ("ret_g", 8), ("ret_out", 8), ("peer_q0", 8),
          ("keys0", 1), ("mla_in_uq", 6), ("mla_k", 1), ("mla_v", 1), ("mla_out", 4), ("peer_q1", 8),
          ("keys1", 1)]
BLOCKS = sum(n for _, n in STREAM)

_COLS = [("g_mix_pre", 8), ("w_dw", 8 * CONV), ("b_dw", 8), ("g_conv_ln", 8), ("b_conv_ln", 8), ("s_pool", 8),
         ("g_mix_post", 8), ("g_ffn_pre", 8), ("g_ffn_post", 8), ("gn_g", 16), ("gn_b", 16), ("q_norm", 3),
         ("kv_norm", 2), ("ln_g0", 8), ("ln_b0", 8), ("ln_g1", 8), ("ln_b1", 8), ("freq_ret", 1),
         ("freq_mla", 1), ("quarter", 4)]
COL, _n = {}, 0
for _name, _w in _COLS:
    COL[_name] = _n
    _n += _w
NCOL = _n


class Chain:

    def __init__(self, eng, sem, plain=None):
        self.eng, self.sem, self.n, self.i, self.per, self.plain = eng, sem, 0, None, 0, plain

    def enter(self, i, per):
        self.i, self.per, self.at = i, per, self.n

    def leave(self, times):
        assert self.n - self.at == self.per, (self.n - self.at, self.per)
        self.n, self.i = self.at + self.per * times, None

    def link(self, ins):
        self.n += 1
        ins.then_inc(self.sem, 1)
        self.eng.wait_ge(self.sem, self.n if self.i is None else self.n + self.i * self.per)

    def link_alone(self, ins):
        self.link(ins)
        if self.i is not None:
            self.eng.sem_inc(self.plain, 1)


class Turns:

    def __init__(self, eng, full, free, banks, plain=None):
        self.plain = plain
        self.eng, self.full, self.free, self.banks, self.n, self.i = eng, full, free, banks, 0, None

    def enter(self, i, per):
        self.i, self.at, self.per = i, self.n, per

    def leave(self, times):
        assert self.n - self.at == self.per == BANKS
        self.n, self.i = self.at + BANKS * times, None

    def wait(self, sem, count):
        if self.i is None:
            if count > 0:
                self.eng.wait_ge(sem, count)
        else:
            self.eng.wait_ge(sem, count + self.i)

    def bank(self):
        return self.banks[self.n % BANKS]

    def wait_full(self):
        self.wait(self.full[self.n % BANKS], self.n // BANKS + 1)

    def wait_full_alone(self):
        self.wait_full()
        if self.i is not None:
            self.eng.sem_inc(self.plain, 1)

    def wait_free(self):
        self.wait(self.free[self.n % BANKS], self.n // BANKS)

    def wait_stored(self, use):
        self.wait(self.free[use % BANKS], use // BANKS + 1)

    def release(self, ins):
        ins.then_inc(self.free[self.n % BANKS], 1)
        self.n += 1

    def filled(self, ins):
        ins.then_inc(self.full[self.n % BANKS], 1)
        self.n += 1


@contextmanager
def repeat(eng, times, *counters):
    with eng.Fori(0, times) as i:
        for c, per in counters:
            c.enter(i, per)
        yield i
    for c, _ in counters:
        c.leave(times)


def build(nc, stream, cols, rows, x_cm, p_cm, sgu_wt, rcnt_in, positions, decay, uv0, uv1, out, stop=None):
    ctx = ExitStack()
    with ctx:
        def sb(name, shape, dt=FP32):
            return ctx.enter_context(nc.sbuf_tensor(name, shape, dt))

        def sem(name):
            return ctx.enter_context(nc.semaphore(name))

        WR = sb("w_ring", [P, SLOTS, TILES, P])
        CO = sb("channel_vectors", [P, NCOL])
        RO = sb("row_vectors", [P, 3, D])
        IDENT = sb("ident", [P, P])
        ALPHA_I = sb("alpha_ident", [P, P])
        ZERO = sb("zero_square", [P, P])
        ONES = sb("ones", [P, P])
        X0 = sb("x0", [P, KT, S])
        X1 = sb("x1", [P, KT, S])
        SC = sb("scratch", [P, KT, S])
        MU = sb("mu", [P, S])
        RS = sb("rstd", [P, S])
        AR = sb("arena", [P, 120 * S])

        def region(tile, n, t=S, dt=None):
            a = AR[:, int(tile * S):int(tile * S) + n * t].rearrange("p (k t) -> p k t", t=t)
            return a if dt is None else a.bitcast(dt)

        PADH = region(0, KT, PAD + S)
        CV = region(9, KT)
        PADZ = region(17, KT, ZPAD + S)
        PA = region(26, 2, ZPAD + S)
        PB = region(28.5, 2, ZPAD + S)
        POOLED = region(31, KT)
        POOLMIX = region(39, KT)
        U = region(47, KT)
        VT = region(55, TT, D)
        AIN = region(63, KT)
        GATES = region(71, 3 * KT)
        MERGED = region(95, KT)
        RC = region(103, 4)
        SG = region(107, 4)
        WS = AR[:, 111 * S:115 * S].rearrange("p (h i) -> p h i", i=P)
        PT = region(115, 2)
        F = region(0, FT)
        MO = region(31, KT)
        PL = region(39, KT)
        QK = region(0, 16)
        V = region(16, TT, 2048)
        GS = region(32, 16)
        DEC = region(48, 8)
        PR = region(56, 8)
        YN = region(64, 8, RET_DV)
        YG = region(80, 16)
        COS, SIN = region(96, 2), region(98, 2)
        RA, RB = region(100, 2), region(102, 2)
        DIFF = region(104, 2)
        DNEG = region(106, 2)
        POSF = region(108, 1)
        ANG = region(109, 1)
        TURN = region(110, 1)
        POSI = region(111, 1, dt=I32)
        DIFI = region(112, 2, dt=I32)
        DC = sb("decay_rates", [P, 5, 2 * RET_HEADS])
        CC = region(0, 7)
        CN = region(7, 5)
        KR = region(12, 2)
        QN = region(14, 12)
        QR = region(82, 4)
        KN = region(26, KT)
        VM = region(34, TT, D)
        PS = region(42, 2 * MLA_HEADS)
        PTT = region(58, 2 * MLA_HEADS)
        OM = region(74, MLA_HEADS)
        KRM = region(86, 8)
        G = region(0, 8, 2 * D)
        SCO = region(64, 2 * HEADS * TT, NKEYS)
        QT = region(80, 16)
        HTM = region(101, TT, D)
        DG = region(109, 8, P)
        SK = region(113, 2, NKEYS)
        SL = region(114, 2, NKEYS)
        CA = region(115, 1)
        CB = region(116, 1)
        OH = region(117, 2)
        IOTA16 = sb("iota16", [P, TOPK])
        IOTAI = sb("iota16_int", [P, TOPK], I32)
        M16 = sb("top_per_side", [P, 2, TOPK])
        I16 = sb("index_per_side", [P, 2, TOPK], U32)
        IF16 = sb("index_per_side_float", [P, 2, TOPK])
        T16 = sb("top_pairs", [P, TOPK])
        P16 = sb("place_of_pairs", [P, TOPK], U32)
        AB = sb("place_halves", [P, 2, TOPK], U32)
        ABF = sb("place_halves_float", [P, 2, TOPK])
        EI = sb("expert_halves", [P, 2, TOPK])
        EIDX = sb("expert_index", [P, 2, TOPK], I32)
        NM = sb("minus_top", [P, 1])
        EX = sb("exp_top", [P, 2, TOPK])
        ES = sb("exp_sum", [P, 2])
        GT = sb("gate", [P, 2, TOPK])
        HD = sb("dots", [P, 2, 4])
        GL = sb("gelu_dots", [P, 2, 4])
        WT = sb("expert_weights", [P, 2, 4])
        BN = sb("bn_parts", [P, 2, 6])
        MV = sb("mean_var", [P, 2])
        RT = sb("rstd_tokens", [P, 1])
        MX = sb("score_max", [P, MLA_HEADS, 2])
        SU = sb("prob_sum", [P, MLA_HEADS, 2])

        def psum(name):
            return ctx.enter_context(nc.psum_tensor(name, [P, 512], FP32))

        ACC = [psum(f"acc{i}") for i in range(BANKS)]
        AUX = [psum(f"aux{i}") for i in range(4)]

        def halves(bank):
            return bank[:, :].rearrange("p (a t) -> p a t", a=2)

        def col(name, k=0, n=1):
            return CO[:, COL[name] + k:COL[name] + k + n]

        w_full = [sem(f"w_full{i}") for i in range(SLOTS)]
        w_free = [sem(f"w_free{i}") for i in range(SLOTS)]
        acc_full = [sem(f"acc_full{i}") for i in range(BANKS)]
        acc_free = [sem(f"acc_free{i}") for i in range(BANKS)]
        act_chain, dve_chain, pool_chain = sem("act_chain"), sem("dve_chain"), sem("pool_chain")
        x_loaded, cols_loaded, rows_loaded = sem("x_loaded"), sem("cols_loaded"), sem("rows_loaded")
        small_loaded, sgu_w_loaded, pos_loaded = sem("small_loaded"), sem("sgu_w_loaded"), sem("pos_loaded")
        p_loaded = sem("p_loaded")
        ones_ready, ident_ready, pads_ready = sem("ones_ready"), sem("ident_ready"), sem("pads_ready")
        squares_ready = sem("squares_ready")
        sums_ready = sem("sums_ready")
        var_ready = sem("var_ready")
        root_ready = sem("root_ready")
        centred = sem("centred")
        input_ready = sem("input_ready")
        input_ready_act = sem("input_ready_act")
        scaled = sem("scaled")
        gate_half = sem("gate_half")
        pooled_ready = sem("pooled_ready")
        sgu_w_ready = sem("sgu_w_ready")
        mix_ready = sem("mix_ready")
        ple_gated = sem("ple_gated")
        freq_act, freq_dve = sem("freq_act"), sem("freq_dve")
        iota_ready = sem("iota_ready")
        scores_ready, probs_ready = sem("scores_ready"), sem("probs_ready")
        y_ready, yn_ready = sem("y_ready"), sem("yn_ready")
        gained = sem("gained")
        mla_scored, mla_max, mla_exp, mla_prob = sem("mla_scored"), sem("mla_max"), sem("mla_exp"), sem("mla_prob")
        mla_turned, mla_probs_cm = sem("mla_turned"), sem("mla_probs_cm")
        waits_passed = sem("waits_passed")
        idx_ready = sem("idx_ready")
        top_ready = sem("top_ready")
        exp_ready = sem("exp_ready")
        gathered = [sem(f"gathered{i}") for i in range(8)]
        half_free = sem("half_free")
        dots_ready, gelu_ready = sem("dots_ready"), sem("gelu_ready")
        weights_ready, diag_ready = sem("weights_ready"), sem("diag_ready")
        experts_summed = sem("experts_summed")
        tokens_normed = sem("tokens_normed")
        rows_free = sem("rows_free")
        stored = sem("stored")

        block = ctx.enter_context(nc.Block())

        @block.sync
        def _(sp):
            for s in range(SLOTS):
                sp.dma_start(WR[:, s, :, :], stream[s]).then_inc(w_full[s], 16)
            groups = BLOCKS // SLOTS

            def send(g, s):
                sp.wait_ge(w_free[s], g + 1 if s == SLOTS - 1 else g)
                sp.dma_start(WR[:, s, :, :], stream[bass.ds(SLOTS * g + s, 1)].rearrange("o p a b -> p (o a) b")
                             if not isinstance(g, int) else stream[SLOTS * g + s]).then_inc(w_full[s], 16)

            with sp.Fori(1, groups) as g:
                for s in range(SLOTS):
                    send(g, s)
            for s in range(BLOCKS % SLOTS):
                send(groups, s)
            if stop:
                return
            for tt in range(TT):
                sp.wait_ge(tokens_normed, TT + tt + 1)
                sp.dma_start(out[0, tt * P:(tt + 1) * P, :], HTM[:, tt, :]).then_inc(stored, 16)
            sp.wait_ge(stored, 16 * TT)

        @block.tensor
        def _(pe):
            t = [0]
            ring = Turns(pe, acc_full, acc_free, ACC)
            n = dict(squares=0, inp=0, inp_act=0)

            def tile(i, width=1):
                b, at = divmod(t[0], TILES)
                first = at == 0
                if first:
                    if i is None:
                        pe.wait_ge(w_full[b % SLOTS], 16 * (b // SLOTS + 1))
                    else:
                        pe.wait_ge(w_full[b % SLOTS], 16 * (b // SLOTS + 1) + i * 16)
                t[0] += width
                w = WR[:, b % SLOTS, at:at + width, :]
                return w, ((b - 1) % SLOTS if first else None)

            def entered(ins, slot):
                if slot is not None:
                    ins.then_inc(w_free[slot], 1)

            def pairs(x, kt, tiles, i=None):
                for o in range(tiles):
                    if o % 2 == 0:
                        ring.wait_free()
                    bank = ring.bank()
                    for k in range(kt):
                        w, slot = tile(i)
                        last = nc.tensor.matmul(bank[:, (o % 2) * S:(o % 2 + 1) * S], w[:, 0, :], x[:, k, :],
                                                start=(k == 0), stop=(k == kt - 1))
                        entered(last, slot)
                    if o % 2 or o == tiles - 1:
                        ring.filled(last)

            def token_major(x, kt, chunks, i=None):
                for _ in range(chunks):
                    ring.wait_free()
                    at, b0 = ring.n, ring.bank()
                    ring.n += 1
                    ring.wait_free()
                    b1 = ring.bank()
                    ring.n = at
                    for k in range(kt):
                        w, slot = tile(i, 4)
                        w = w.rearrange("p a b -> p (a b)")
                        for tt, bank in enumerate((b0, b1)):
                            last = nc.tensor.matmul(bank[:, :], x[:, k, tt * P:(tt + 1) * P], w,
                                                    start=(k == 0), stop=(k == kt - 1))
                            if tt == 0:
                                entered(last, slot)
                                if k == kt - 1:
                                    ring.filled(last)
                    ring.filled(last)

            def loop(fn, times, *args):
                t0 = t[0]
                with repeat(pe, times, (ring, BANKS)) as i:
                    fn(*args, i=i)
                assert t[0] - t0 == SLOTS * TILES
                t[0] = t0 + SLOTS * TILES * times

            def need_input():
                n["inp"] += 1
                pe.wait_ge(input_ready, n["inp"])

            def need_input_act():
                n["inp_act"] += 1
                pe.wait_ge(input_ready_act, n["inp_act"])

            def stored_by_evacuation(uses=BANKS):
                for u in range(ring.n - uses, ring.n):
                    ring.wait_stored(u)

            def channel_sums(x, kt, half=0, per=None):
                for k in range(kt):
                    if per and k % per == 0:
                        n["squares"] += 1
                        pe.wait_ge(squares_ready, n["squares"])
                    last = nc.tensor.matmul(AUX[3 - half][:, 0:S], ONES[:, :], x[:, k, :],
                                            start=(k == 0), stop=(k == kt - 1))
                last.then_inc(sums_ready, 1)

            def square_sums(x=SC, kt=KT, half=0, per=None):
                channel_sums(x, kt, half, per or kt)

            pe.wait_ge(ones_ready, 1)
            square_sums()
            need_input()
            pairs(X1, KT, 8)
            pairs(X1, KT, 8)
            pairs(X1, KT, 8)
            pairs(X1, KT, 8)
            token_major(X1, KT, 2)
            need_input()
            channel_sums(CV, KT)
            pairs(X1, KT, 8)
            square_sums(half=1)
            loop(pairs, 2, X1, KT, 8)
            pe.wait_ge(pooled_ready, 1)
            for g in range(4):
                pairs(POOLED[:, 2 * g:2 * g + 2, :], 2, 2)
            need_input()
            pe.wait_ge(sgu_w_ready, 1)
            for h in range(8):
                for b in range(TT):
                    c = (h % 2) * S + b * P
                    last = nc.tensor.matmul(AUX[h // 2][:, c:c + P], VT[:, b, h * P:(h + 1) * P], WS[:, h, :],
                                            start=True, stop=True)
                if h % 2:
                    last.then_inc(mix_ready, 1)
            need_input_act()
            pairs(CV, KT, 8)
            pairs(POOLMIX, KT, 8)
            need_input()
            pairs(AIN, KT, 8)
            need_input()
            pairs(MERGED, KT, 8)
            square_sums(per=2)
            square_sums(per=2)
            need_input()
            loop(pairs, 5, X1, KT, 8)
            pairs(X1, KT, 4)
            stored_by_evacuation()
            pairs(F, FT, 8)
            pe.wait_ge(p_loaded, 16)
            pairs(PT, 2, 8)
            square_sums(per=2)
            need_input()
            pairs(X0, KT, 8)
            if stop == "first":
                return
            need_input()
            loop(pairs, 2, X1, KT, 8)
            loop(token_major, 2, X1, KT, 2)
            need_input()
            for e in range(RET_HEADS):
                for mt in range(TT):
                    for d in range(2):
                        last = nc.tensor.matmul(AUX[e][:, mt * S:(mt + 1) * S],
                                                QK[:, 8 + 2 * e + d, mt * P:(mt + 1) * P], QK[:, 2 * e + d, :],
                                                start=(d == 0), stop=(d == 1))
                last.then_inc(scores_ready, 1)
            stored_by_evacuation()
            loop(pairs, 2, X1, KT, 8)
            pe.wait_ge(probs_ready, RET_HEADS)

            def weigh(e):
                if e >= 2:
                    pe.wait_ge(yn_ready, 2 * (e - 1))
                for nt in range(TT):
                    for mt in range(TT):
                        last = nc.tensor.matmul(AUX[2 * (e % 2) + nt][:, :],
                                                PR[:, 2 * e + mt, nt * P:(nt + 1) * P],
                                                V[:, mt, e * RET_DV:(e + 1) * RET_DV], start=(mt == 0), stop=(mt == 1))
                    last.then_inc(y_ready, 1)

            def turn(e):
                pe.wait_ge(yn_ready, 2 * (e + 1))
                for c in range(4):
                    if c % 2 == 0:
                        ring.wait_free()
                    for nt in range(TT):
                        at = (c % 2) * S + nt * P
                        last = nc.tensor.transpose(ring.bank()[:, at:at + P], YN[:, 2 * e + nt, c * P:(c + 1) * P],
                                                   IDENT[:, :])
                    if c % 2:
                        ring.filled(last)

            weigh(0)
            weigh(1)
            turn(0)
            weigh(2)
            turn(1)
            weigh(3)
            turn(2)
            turn(3)
            need_input()
            pairs(YG, 16, 8)
            need_input()
            channel_sums(X0, KT)
            square_sums(half=1)

            def peer(layer):
                need_input_act()
                loop(pairs, 2, X0, KT, 8)
                for tt in range(TT):
                    for half in range(2):
                        ring.wait_free()
                        for k in range(4):
                            last = nc.tensor.transpose(ring.bank()[:, k * P:(k + 1) * P],
                                                       X0[:, 4 * half + k, tt * P:(tt + 1) * P], IDENT[:, :])
                        ring.filled(last)
                stored_by_evacuation(2 * BANKS)
                tile0 = t[0]
                for tt in range(TT):
                    t[0] = tile0
                    for j in range(2 * HEADS):
                        if j % 4 == 0:
                            ring.wait_free()
                        w, slot = tile(None)
                        last = nc.tensor.matmul(ring.bank()[:, (j % 4) * P:(j % 4 + 1) * P],
                                                QT[:, j, tt * P:(tt + 1) * P], w[:, 0, :], start=True, stop=True)
                        if tt == 0:
                            entered(last, slot)
                        if j % 4 == 3:
                            ring.filled(last)
                for tt in range(TT):
                    for c in range(2):
                        last = nc.tensor.matmul(AUX[2 * tt + c][:, :], ALPHA_I[:, :], HTM[:, tt, c * 512:(c + 1) * 512],
                                                start=True, stop=False)
                    last.then_inc(half_free, 1)

            def experts(layer):
                base = layer * (TT * HEADS * 4)
                for tt in range(TT):
                    def units(i, tt=tt):
                        for q in range(8):
                            b = base + tt * HEADS * 4 + q
                            pe.wait_ge(diag_ready, b + 1 + i * 8)
                            for s in range(4):
                                for c in range(2):
                                    last = nc.tensor.matmul(AUX[2 * tt + c][:, :], DG[:, (q % 2) * 4 + s, :],
                                                            G[:, (q % 2) * 4 + s, D + c * 512:D + (c + 1) * 512],
                                                            start=False, stop=False)
                            last.then_inc(half_free, 1)
                    with pe.Fori(0, HEADS // 2) as i:
                        units(i)
                    for c in range(2):
                        last = nc.tensor.matmul(AUX[2 * tt + c][:, :], ZERO[:, :], HTM[:, tt, c * 512:(c + 1) * 512],
                                                start=False, stop=True)
                    last.then_inc(experts_summed, 1)

            peer(0)
            experts(0)
            pe.wait_ge(tokens_normed, TT)
            for s in range(4):
                ring.wait_free()
                for k in range(2):
                    for tt in range(TT):
                        at = k * S + tt * P
                        last = nc.tensor.transpose(ring.bank()[:, at:at + P], HTM[:, tt, (2 * s + k) * P:(2 * s + k + 1) * P],
                                                   IDENT[:, :])
                ring.filled(last)
            stored_by_evacuation()
            pairs(X1, KT, 7)
            square_sums(kt=3)
            square_sums(SC[:, 3:5, :], kt=2, half=1)
            need_input()
            pairs(CN, 3, 12)
            t[0] += 4
            pairs(CN[:, 3:5, :], 2, 8)
            token_major(CN[:, 3:5, :], 2, 2)
            need_input()
            stored_by_evacuation(8)

            def score(e):
                if e >= 2:
                    pe.wait_ge(mla_exp, 2 * (e - 1))
                for qt in range(TT):
                    o = AUX[e % 2][:, qt * S:(qt + 1) * S]
                    nc.tensor.matmul(o, QN[:, e, qt * P:(qt + 1) * P], KN[:, e, :], start=True, stop=False)
                    nc.tensor.matmul(o, QR[:, e // 4, qt * P:(qt + 1) * P], KRM[:, e % 4, :], start=False, stop=False)
                    last = nc.tensor.matmul(o, QR[:, 2 + e // 4, qt * P:(qt + 1) * P], KRM[:, 4 + e % 4, :],
                                            start=False, stop=True)
                last.then_inc(mla_scored, 1)

            def turn_probs(e):
                pe.wait_ge(mla_prob, e + 1)
                if e >= 2:
                    pe.wait_ge(mla_probs_cm, e - 1)
                for kt in range(TT):
                    for qt in range(TT):
                        at = kt * S + qt * P
                        last = nc.tensor.transpose(AUX[2 + e % 2][:, at:at + P], PS[:, 2 * e + qt, kt * P:(kt + 1) * P],
                                                   IDENT[:, :])
                last.then_inc(mla_turned, 1)

            def weigh_values(e):
                pe.wait_ge(mla_probs_cm, e + 1)
                if e % 2 == 0:
                    ring.wait_free()
                for kt in range(TT):
                    last = nc.tensor.matmul(ring.bank()[:, (e % 2) * S:(e % 2 + 1) * S], VM[:, kt, e * P:(e + 1) * P],
                                            PTT[:, 2 * e + kt, :], start=(kt == 0), stop=(kt == 1))
                if e % 2:
                    ring.filled(last)

            for e in range(MLA_HEADS + 2):
                if e < MLA_HEADS:
                    score(e)
                if 0 <= e - 1 < MLA_HEADS:
                    turn_probs(e - 1)
                if e >= 2:
                    weigh_values(e - 2)
            stored_by_evacuation()
            pairs(OM, MLA_HEADS, 8)
            need_input()
            channel_sums(X0, KT)
            square_sums(half=1)
            peer(1)
            experts(1)
            assert t[0] == BLOCKS * TILES, (t[0], BLOCKS * TILES)

        @block.gpsimd
        def _(pool):
            chain = Chain(pool, pool_chain)
            link = chain.link
            nc.gpsimd.memset(ONES[:, :], 1.0).then_inc(ones_ready, 1)
            nc.gpsimd.memset(PADH[:, :, 0:PAD], 0.0)
            nc.gpsimd.memset(PADZ[:, :, 0:ZPAD], 0.0).then_inc(pads_ready, 1)
            link(nc.gpsimd.memset(IDENT[:, :], 1.0))
            link(nc.gpsimd.affine_select(out=IDENT[:, :], in_=IDENT[:, :], pattern=[[-1, P]],
                                         compare_op=ALU.is_equal, fill=0.0, base=0, channel_multiplier=1))
            nc.gpsimd.memset(ZERO[:, :], 0.0)
            link(nc.gpsimd.memset(ALPHA_I[:, :], ALPHA))
            nc.gpsimd.affine_select(out=ALPHA_I[:, :], in_=ALPHA_I[:, :], pattern=[[-1, P]],
                                    compare_op=ALU.is_equal, fill=0.0, base=0,
                                    channel_multiplier=1).then_inc(ident_ready, 1)
            link(nc.gpsimd.iota(IOTAI[:, :], pattern=[[1, TOPK]], base=0, channel_multiplier=0))
            link(nc.gpsimd.tensor_copy(IOTA16[:, :], IOTAI[:, :]))
            pool.sem_inc(iota_ready, 1)
            pool.wait_ge(sgu_w_loaded, 16)
            link(nc.gpsimd.memset(WS[P // 2:P, :, 0:P // 2], 0.0))
            pool.sem_inc(sgu_w_ready, 1)
            pool.wait_ge(small_loaded, 16)
            for u in range(8, 12):
                pool.wait_ge(acc_free[u % BANKS], u // BANKS + 1)
            for g in range(len(WINDOWS)):
                src, lo = PADZ[:, 2 * g:2 * g + 2, :], 0
                for n in range(g + 1):
                    dst, step = (PA, PB)[n % 2], 2 ** n
                    lo += step
                    link(nc.gpsimd.tensor_tensor(dst[:, :, lo:ZPAD + S], src[:, :, lo:ZPAD + S],
                                                 src[:, :, lo - step:ZPAD + S - step], ALU.add))
                    src = dst
                link(nc.gpsimd.tensor_tensor(POOLED[:, 2 * g:2 * g + 2, :], src[:, :, ZPAD:ZPAD + S],
                                             RC[:, g:g + 1, :].broadcast_to([P, 2, S]), ALU.mult))
                last = nc.gpsimd.tensor_tensor(POOLED[:, 2 * g:2 * g + 2, :], POOLED[:, 2 * g:2 * g + 2, :],
                                               PADZ[:, 2 * g:2 * g + 2, ZPAD:ZPAD + S], ALU.subtract)
                link(last) if g < 3 else last.then_inc(pooled_ready, 1)
            if stop == "first":
                return
            pool.wait_ge(input_ready, 8)
            nc.gpsimd.iota(DIFI, pattern=[[-P, 2], [1, S]], base=0, channel_multiplier=-1).then_inc(iota_ready, 1)
            for layer in range(2):
                uv = (uv0, uv1)[layer]
                for tt in range(TT):
                    base = layer * (TT * HEADS * 4) + tt * HEADS * 4
                    with pool.Fori(0, HEADS // 2) as i:
                        for q in range(8):
                            pool.wait_ge(half_free, 2 * layer + base + q + 1 + i * 8)
                            if q % 4 == 0:
                                unit = base // 4 + q // 4
                                pool.wait_ge(idx_ready, unit + 1 + i * 2)
                            pool.sem_inc(waits_passed, 1)
                            for s in range(4):
                                slot = (q % 2) * 4 + s
                                pool.indirect_dma_start(
                                    G[:, slot, :], None, uv,
                                    bass.IndirectOffsetOnAxis(ap=EIDX[:, q // 4, (q % 4) * 4 + s:(q % 4) * 4 + s + 1], axis=0),
                                ).then_inc(gathered[slot], 16)

        @block.scalar
        def _(act):
            chain = Chain(act, act_chain)
            link = chain.link
            ring = Turns(act, acc_full, acc_free, ACC, waits_passed)
            n = dict(centred=0, scaled=0, roots=0)
            act.dma_start(X0[:, :, :], x_cm).then_inc(x_loaded, 16)
            act.dma_start(CO[:, :], cols).then_inc(cols_loaded, 16)
            act.dma_start(RO[:, 0:3, :], rows[0:3].partition_broadcast(P)).then_inc(rows_loaded, 16)
            act.dma_start(RC, rcnt_in.partition_broadcast(P)).then_inc(small_loaded, 16)
            act.dma_start(WS, sgu_wt).then_inc(sgu_w_loaded, 16)
            act.dma_start(PT, p_cm).then_inc(p_loaded, 16)

            def evacuate(func, dst, scale=1.0):
                ring.wait_full_alone()
                ring.release(nc.scalar.activation(dst, halves(ring.bank()), func, scale=scale))

            def evacuate_tm(func, dst):
                ring.wait_full_alone()
                ring.release(nc.scalar.activation(dst, ring.bank()[:, :], func))

            def root(x, times=1):
                for _ in range(times):
                    n["roots"] += 1
                    act.wait_ge(var_ready, n["roots"])
                    nc.scalar.activation(x[:, :], x[:, :], ACT.Sqrt).then_inc(root_ready, 1)

            def square(dst, src):
                n["centred"] += 1
                act.wait_ge(centred, n["centred"])
                nc.scalar.activation(dst, src, ACT.Square).then_inc(squares_ready, 1)

            def gain_bias(dst, src, g, b, func=ACT.Identity):
                n["scaled"] += 1
                act.wait_ge(scaled, n["scaled"])
                for k in range(KT):
                    last = nc.scalar.activation(dst[:, k, :], src[:, k, :], func, bias=col(b, k), scale=col(g, k))
                last.then_inc(input_ready_act, 1)

            act.wait_ge(x_loaded, 16)
            nc.scalar.activation(SC[:, :, :], X0[:, :, :], ACT.Square).then_inc(squares_ready, 1)
            root(RS)
            with repeat(act, 2, (ring, BANKS)):
                for s in range(BANKS):
                    ring.wait_full()
                    nc.scalar.activation(SG[:, s, :], ring.bank()[:, S:2 * S], ACT.Sigmoid).then_inc(gate_half, 1)
                    ring.n += 1
            act.wait_ge(pads_ready, 1)
            for s in range(4):
                evacuate(ACT.Copy, PADZ[:, 2 * s:2 * s + 2, ZPAD:ZPAD + S])
            for s in range(4):
                evacuate(ACT.Gelu_apprx_tanh, U[:, 2 * s:2 * s + 2, :])
            for c in range(2):
                for tt in range(TT):
                    evacuate_tm(ACT.Gelu_apprx_tanh, VT[:, tt, c * 512:(c + 1) * 512])
            for s in range(4):
                evacuate(ACT.Sigmoid, GATES[:, 2 * s:2 * s + 2, :])
            square(SC[:, :, :], CV)
            root(RS)
            root(RT, TT)
            with repeat(act, 2, (ring, BANKS)) as i:
                for s in range(BANKS):
                    evacuate(ACT.Sigmoid, GATES[:, bass.ds(8 + 2 * s + i * 8, 2), :])
            for s in range(4):
                ring.wait_full()
                act.wait_ge(cols_loaded, 16)
                nc.scalar.activation(POOLMIX[:, 2 * s, :], ring.bank()[:, 0:S], ACT.Copy, scale=col("s_pool", 2 * s))
                ring.release(nc.scalar.activation(POOLMIX[:, 2 * s + 1, :], ring.bank()[:, S:2 * S], ACT.Copy,
                                                  scale=col("s_pool", 2 * s + 1)))
            gain_bias(CV, CV, "g_conv_ln", "b_conv_ln", ACT.Silu)
            ring.n += 12
            def squares_by_pair(src):
                for s in range(4):
                    square(SC[:, 2 * s:2 * s + 2, :], src[:, 2 * s:2 * s + 2, :])

            def squares_of_copies():
                for s in range(4):
                    ring.wait_stored(ring.n)
                    ring.n += 1
                    nc.scalar.activation(SC[:, 2 * s:2 * s + 2, :], MO[:, 2 * s:2 * s + 2, :], ACT.Square)\
                      .then_inc(squares_ready, 1)

            squares_of_copies()
            root(RS)
            squares_by_pair(X0)
            root(RS)
            with repeat(act, 5, (ring, BANKS)):
                for s in range(BANKS):
                    ring.wait_full()
                    nc.scalar.activation(SG[:, s, :], ring.bank()[:, 0:S], ACT.Silu).then_inc(gate_half, 1)
                    ring.n += 1
            for s in range(2):
                ring.wait_full()
                nc.scalar.activation(SG[:, s, :], ring.bank()[:, 0:S], ACT.Silu).then_inc(gate_half, 1)
                ring.n += 1
            squares_of_copies()
            for s in range(4):
                evacuate(ACT.Copy, PL[:, 2 * s:2 * s + 2, :])
            root(RS)
            for s in range(4):
                ring.wait_full()
                if s >= 2:
                    act.wait_ge(ple_gated, s - 1)
                ring.release(nc.scalar.activation(SG[:, 2 * (s % 2):2 * (s % 2) + 2, :], halves(ring.bank()), ACT.Sigmoid))
            if stop == "first":
                act.wait_ge(ple_gated, 4)
                act.dma_start(out.rearrange("o t d -> (o t d)").rearrange("(p k t) -> p k t", p=P, k=KT), X1[:, :, :]).then_inc(stored, 16)
                act.wait_ge(stored, 16)
                return
            act.wait_ge(ple_gated, 4)
            act.dma_start(POSI[:, 0, :], positions.partition_broadcast(P)).then_inc(pos_loaded, 16)
            act.dma_start(DC[:, 0, :], decay.partition_broadcast(P)).then_inc(pos_loaded, 16)
            act.wait_ge(pos_loaded, 32)
            link(nc.scalar.activation(DC[:, 1, :], DC[:, 0, :], ACT.Exp))
            link(nc.scalar.activation(DC[:, 2, :], DC[:, 1, :], ACT.Identity, scale=-1.0, bias=1.0))
            nc.scalar.activation(DC[:, 3, :], DC[:, 2, :], ACT.Ln).then_inc(freq_act, 1)
            for e in range(RET_HEADS):
                act.wait_ge(freq_dve, e + 1)
                nc.scalar.activation(DEC[:, 2 * e:2 * e + 2, :], DEC[:, 2 * e:2 * e + 2, :], ACT.Exp).then_inc(freq_act, 1)
            for f in range(2):
                act.wait_ge(freq_dve, RET_HEADS + f + 1)
                nc.scalar.activation(SIN[:, f, :], SIN[:, f, :], ACT.Sin)
                nc.scalar.activation(COS[:, f, :], COS[:, f, :], ACT.Sin).then_inc(freq_act, 1)
            ring.n += 8
            with repeat(act, 2, (ring, BANKS)) as i:
                for c in range(2):
                    for tt in range(TT):
                        evacuate_tm(ACT.Copy, V[:, tt, bass.ds(c * 512 + i * 1024, 512)])
            with repeat(act, 2, (ring, BANKS)) as i:
                for s in range(BANKS):
                    evacuate(ACT.Silu, GS[:, bass.ds(2 * s + i * 8, 2), :])
            def gain_heads(e):
                for c in (2 * e, 2 * e + 1):
                    ring.wait_full()
                    nc.scalar.activation(YG[:, 2 * c, :], ring.bank()[:, 0:S], ACT.Identity,
                                         bias=col("gn_b", 2 * c), scale=col("gn_g", 2 * c))
                    ring.release(nc.scalar.activation(YG[:, 2 * c + 1, :], ring.bank()[:, S:2 * S], ACT.Identity,
                                                      bias=col("gn_b", 2 * c + 1), scale=col("gn_g", 2 * c + 1)))

            root(RT, TT)
            root(RT, TT)
            gain_heads(0)
            root(RT, TT)
            gain_heads(1)
            root(RT, TT)
            gain_heads(2)
            gain_heads(3)
            ring.n += 4

            def peer(layer):
                square(SC[:, :, :], X0[:, :, :])
                root(RS)
                gain_bias(X0, X0, f"ln_g{layer}", f"ln_b{layer}")
                if layer:
                    act.wait_ge(tokens_normed, TT)
                act.dma_start(RO[:, 0:2, :], rows[3 + 2 * layer:5 + 2 * layer].partition_broadcast(P)).then_inc(rows_loaded, 16)
                with repeat(act, 2, (ring, BANKS)) as i:
                    for s in range(BANKS):
                        evacuate(ACT.Copy, QT[:, bass.ds(2 * s + i * 8, 2), :])
                ring.n += 4
                for s in range(8):
                    ring.wait_full()
                    ring.release(nc.scalar.activation(SCO[:, 4 * s:4 * s + 4, :],
                                                      ring.bank()[:, :].rearrange("p (a t) -> p a t", t=P), ACT.Copy))
                units0, b0 = layer * TT * HEADS, layer * TT * HEADS * 4

                def exps(par, u, i):
                    act.wait_ge(top_ready, u if i is None else u + i * 2)
                    nc.scalar.activation(EX[:, par, :], T16[:, :], ACT.Exp, bias=NM[:, 0:1],
                                         accum_out=ES[:, par:par + 1]).then_inc(exp_ready, 1)

                def batch(q, b, i):
                    act.wait_ge(dots_ready, b + 1 + i * 8)
                    nc.scalar.activation(GL[:, q % 2, :], HD[:, q % 2, :], ACT.Gelu).then_inc(gelu_ready, 1)
                    act.wait_ge(half_free, 2 * layer + b + 1 + i * 8)
                    act.wait_ge(weights_ready, b + 1 + i * 8)
                    for s in range(4):
                        last = nc.scalar.activation(DG[:, (q % 2) * 4 + s, :], IDENT[:, :], ACT.Copy,
                                                    scale=WT[:, q % 2, s:s + 1])
                    last.then_inc(diag_ready, 1)

                exps(0, units0 + 1, None)
                for tt in range(TT):
                    loops = HEADS // 2 - tt
                    with act.Fori(0, loops) as i:
                        for q in range(8):
                            batch(q, b0 + tt * HEADS * 4 + q, i)
                            if q % 4 == 0:
                                exps(1 - q // 4, units0 + tt * HEADS + q // 4 + 2, i)
                    if tt == 0:
                        root(RT)
                for q in range(8):
                    batch(q, b0 + (TT * HEADS - 2) * 4 + q, 0)
                    if q == 0:
                        exps(1, units0 + TT * HEADS, None)
                root(RT)

            peer(0)
            for s in range(4):
                evacuate(ACT.Copy, X1[:, 2 * s:2 * s + 2, :])
            for s in range(3):
                evacuate(ACT.Copy, CC[:, 2 * s:2 * s + 2, :])
            ring.wait_full()
            ring.release(nc.scalar.activation(CC[:, 6, :], ring.bank()[:, 0:S], ACT.Copy))
            for u in range(ring.n - 4, ring.n):
                ring.wait_stored(u)
            nc.scalar.activation(SC[:, 0:3, :], CC[:, 0:3, :], ACT.Square).then_inc(squares_ready, 1)
            nc.scalar.activation(SC[:, 3:5, :], CC[:, 3:5, :], ACT.Square).then_inc(squares_ready, 1)
            root(RS, 2)
            for s in range(6):
                evacuate(ACT.Copy, QN[:, 2 * s:2 * s + 2, :])
            for s in range(4):
                evacuate(ACT.Copy, KN[:, 2 * s:2 * s + 2, :])
            for c in range(2):
                for tt in range(TT):
                    evacuate_tm(ACT.Copy, VM[:, tt, c * 512:(c + 1) * 512])

            def probs_exp(e):
                act.wait_ge(mla_max, e + 1)
                for qt in range(TT):
                    nc.scalar.activation(PS[:, 2 * e + qt, :], AUX[e % 2][:, qt * S:(qt + 1) * S], ACT.Exp,
                                         bias=MX[:, e, qt:qt + 1], scale=MLA_SCALE,
                                         accum_out=SU[:, e, qt:qt + 1]).then_inc(mla_exp, 1)

            for e in range(MLA_HEADS + 2):
                if e < MLA_HEADS:
                    probs_exp(e)
                if 0 <= e - 1 < MLA_HEADS:
                    act.wait_ge(mla_turned, e)
                    nc.scalar.activation(PTT[:, 2 * e - 2:2 * e, :], halves(AUX[2 + (e - 1) % 2]), ACT.Copy)\
                      .then_inc(mla_probs_cm, 1)
                if e >= 2 and (e - 2) % 2:
                    evacuate(ACT.Copy, OM[:, e - 3:e - 1, :])
            ring.n += 4
            peer(1)

        @block.vector
        def _(dve):
            chain = Chain(dve, dve_chain, waits_passed)
            link, link_alone = chain.link, chain.link_alone
            ring = Turns(dve, acc_full, acc_free, ACC)
            v = nc.vector
            n = dict(sums=0, roots=0)

            def wide(a, k=KT):
                return a[:, None, :].broadcast_to([P, k, S])

            def sums_done():
                n["sums"] += 1
                dve.wait_ge(sums_ready, n["sums"])

            def rooted(dst, ins):
                n["roots"] += 1
                ins.then_inc(var_ready, 1)
                dve.wait_ge(root_ready, n["roots"])
                link(v.reciprocal(dst, dst))

            def rstd(half, width, eps):
                sums_done()
                rooted(RS[:, :], v.tensor_scalar(RS[:, :], AUX[3 - half][:, 0:S], 1.0 / width, eps,
                                                 ALU.mult, ALU.add))

            def rms_apply(dst, src, g, k0, k1, g0=0):
                for k in range(k0, k1):
                    last = v.scalar_tensor_tensor(dst[:, k, :], src[:, k, :], col(g, k - g0), RS[:, :], ALU.mult, ALU.mult)
                return last

            def centre(x):
                sums_done()
                link(v.tensor_scalar(MU[:, :], AUX[3][:, 0:S], 1.0 / D, None, ALU.mult))
                v.tensor_tensor(x, x, wide(MU), ALU.subtract).then_inc(centred, 1)

            def layer_scale(x, eps):
                rstd(1, D, eps)
                v.tensor_tensor(x, x, wide(RS), ALU.mult).then_inc(scaled, 1)

            dve.wait_ge(cols_loaded, 16)
            dve.wait_ge(x_loaded, 16)
            rstd(0, D, EPS)
            rms_apply(X1, X0, "g_mix_pre", 0, KT).then_inc(input_ready, 1)

            def taps(j):
                w = COL["w_dw"]

                def tap(k):
                    return CO[:, w + CONV * j + k:w + CONV * j + k + 1] if isinstance(j, int) else \
                        CO[:, bass.ds(j * CONV + (w + k), 1)]

                def at(k):
                    return PADH[:, j, k:k + S]

                bias = CO[:, COL["b_dw"] + j:COL["b_dw"] + j + 1] if isinstance(j, int) else \
                    CO[:, bass.ds(j + COL["b_dw"], 1)]
                link(v.tensor_scalar(CV[:, j, :], at(0), tap(0), bias, ALU.mult, ALU.add))
                for k in range(1, CONV):
                    last = v.scalar_tensor_tensor(CV[:, j, :], at(k), tap(k), CV[:, j, :], ALU.mult, ALU.add)
                    link(last)

            dve.wait_ge(pads_ready, 1)
            with repeat(dve, 2, (ring, BANKS), (chain, 2 * CONV)) as i:
                for s in range(BANKS):
                    ring.wait_full()
                    dve.wait_ge(gate_half, s + 1 + i * BANKS)
                    ins = v.tensor_tensor(PADH[:, s + i * BANKS, PAD:PAD + S], ring.bank()[:, 0:S], SG[:, s, :], ALU.mult)
                    ring.release(ins)
                for u in range(ring.n - BANKS, ring.n):
                    ring.wait_stored(u)
                for k in range(2):
                    taps(i * 2 + k)
            with repeat(dve, 4, (chain, CONV)) as i:
                taps(i + 4)
            dve.sem_inc(input_ready, 1)
            centre(CV)
            layer_scale(CV, EPS)
            ring.n += 8
            dve.wait_ge(rows_loaded, 16)
            for u in range(ring.n, ring.n + 4):
                ring.wait_stored(u)
            ring.n += 4
            for tt in range(TT):
                for c in range(2):
                    last = v.bn_stats(BN[:, c, :], VT[:, tt, c * 512:(c + 1) * 512])
                    if c:
                        link(last)
                link(v.bn_aggr(MV[:, :], BN[:, :, :]))
                rooted(RT[:, :], v.tensor_scalar(RT[:, :], MV[:, 1:2], EPS, None, ALU.add))
                link(v.tensor_scalar(VT[:, tt, :], VT[:, tt, :], MV[:, 0:1], RT[:, 0:1], ALU.subtract, ALU.mult))
                link(v.tensor_tensor(VT[:, tt, :], VT[:, tt, :], RO[:, 0, :], ALU.mult))
                last = v.tensor_tensor(VT[:, tt, :], VT[:, tt, :], RO[:, 1, :], ALU.add)
                link(last) if tt == 0 else last.then_inc(input_ready, 1)
            ring.n += 12 + 4
            for s in range(4):
                dve.wait_ge(mix_ready, s + 1)
                o = AIN[:, 2 * s:2 * s + 2, :]
                bias = RO[:, 2, 2 * s * P:(2 * s + 2) * P].rearrange("p (h i) -> p h i", i=P)[:, :, None, :]\
                    .broadcast_to([P, 2, TT, P])
                link(v.tensor_tensor(o.rearrange("p h (b i) -> p h b i", b=TT),
                                     AUX[s][:, :].rearrange("p (h b i) -> p h b i", h=2, b=TT), bias, ALU.add))
                last = v.tensor_tensor(o, o, U[:, 2 * s:2 * s + 2, :], ALU.mult)
            last.then_inc(input_ready, 1)
            for step, g in enumerate((1, 2, 0)):
                for s in range(4):
                    gate = GATES[:, KT * g + 2 * s:KT * g + 2 * s + 2, :]
                    dst = MERGED[:, 2 * s:2 * s + 2, :]
                    ring.wait_full()
                    if step == 0:
                        ring.release(v.tensor_tensor(dst, halves(ring.bank()), gate, ALU.mult))
                        continue
                    tmp = SG[:, 2 * (s % 2):2 * (s % 2) + 2, :]
                    ring.release(v.tensor_tensor(tmp, halves(ring.bank()), gate, ALU.mult))
                    ring.wait_stored(ring.n - 1)
                    last = v.tensor_tensor(dst, dst, tmp, ALU.add)
                    if step == 2 and s == 3:
                        last.then_inc(input_ready, 1)
                    else:
                        link(last)

            def copy_out(dst):
                for s in range(4):
                    ring.wait_full()
                    ring.release(v.tensor_copy(dst[:, 2 * s:2 * s + 2, :], halves(ring.bank())))

            def add_normed(g, signal):
                rstd(0, D, EPS)
                for s in range(4):
                    link(rms_apply(MO, MO, g, 2 * s, 2 * s + 2))
                    last = v.tensor_tensor(X0[:, 2 * s:2 * s + 2, :], X0[:, 2 * s:2 * s + 2, :],
                                           MO[:, 2 * s:2 * s + 2, :], ALU.add)
                    if signal is not None:
                        last.then_inc(signal, 1)
                    else:
                        link(last)

            copy_out(MO)
            add_normed("g_mix_post", centred)
            rstd(0, D, EPS)
            rms_apply(X1, X0, "g_ffn_pre", 0, KT).then_inc(input_ready, 1)
            gh = 8
            with repeat(dve, 5, (ring, BANKS)) as i:
                for s in range(BANKS):
                    ring.wait_full()
                    dve.wait_ge(gate_half, gh + s + 1 + i * BANKS)
                    ring.release(v.tensor_tensor(F[:, s + i * BANKS, :], ring.bank()[:, S:2 * S], SG[:, s, :], ALU.mult))
            for s in range(2):
                ring.wait_full()
                dve.wait_ge(gate_half, gh + 20 + s + 1)
                ring.release(v.tensor_tensor(F[:, 20 + s, :], ring.bank()[:, S:2 * S], SG[:, s, :], ALU.mult))
            copy_out(MO)
            add_normed("g_ffn_post", None)
            dve.sem_inc(input_ready, 1)
            ple0 = ring.n
            ring.n += 4
            for s in range(4):
                ring.wait_stored(ple0 + s)
                ring.wait_stored(ring.n)
                ring.n += 1
                sg = SG[:, 2 * (s % 2):2 * (s % 2) + 2, :]
                t = PL[:, 2 * s:2 * s + 2, :]
                link(v.tensor_tensor(t, t, sg, ALU.mult))
                link(v.tensor_tensor(X1[:, 2 * s:2 * s + 2, :], X0[:, 2 * s:2 * s + 2, :], t, ALU.add))
                dve.sem_inc(ple_gated, 1)
            dve.sem_inc(input_ready, 1)
            if stop == "first":
                return
            dve.wait_ge(iota_ready, 2)
            link(v.tensor_copy(DNEG, DIFI))
            link(v.tensor_scalar(DIFF, DNEG, 0.0, None, ALU.max))
            link(v.tensor_scalar(DNEG, DNEG, 0.0, -1.0, ALU.min, ALU.mult))
            dve.wait_ge(freq_act, 1)
            link(v.tensor_scalar(DC[:, 2, :], DC[:, 2, :], -1.0, 1.0, ALU.mult, ALU.add))
            link(v.tensor_scalar(DC[:, 0, :], DC[:, 2, :], 1e-30, None, ALU.max))
            link(v.reciprocal(DC[:, 0, :], DC[:, 0, :]))
            link(v.tensor_tensor(DC[:, 3, :], DC[:, 3, :], DC[:, 0, :], ALU.mult))
            link(v.tensor_tensor(DC[:, 3, :], DC[:, 3, :], DC[:, 1, :], ALU.mult))
            link(v.tensor_scalar(DC[:, 4, :], DC[:, 2, :], 0.0, None, ALU.is_equal))
            link(v.tensor_tensor(DC[:, 4, :], DC[:, 4, :], DC[:, 1, :], ALU.mult))
            link(v.tensor_tensor(DC[:, 3, :], DC[:, 3, :], DC[:, 4, :], ALU.subtract))
            for e in range(RET_HEADS):
                dst = DEC[:, 2 * e:2 * e + 2, :]
                link(v.tensor_scalar(dst, DIFF, DC[:, 3, e:e + 1], None, ALU.mult))
                v.scalar_tensor_tensor(dst, DNEG, DC[:, 3, RET_HEADS + e:RET_HEADS + e + 1], dst, ALU.mult, ALU.add)\
                 .then_inc(freq_dve, 1)
            dve.wait_ge(pos_loaded, 32)
            link(v.tensor_copy(POSF, POSI))
            for f, name in enumerate(("freq_ret", "freq_mla")):
                link(v.tensor_scalar(ANG, POSF, col(name), None, ALU.mult))
                link(v.tensor_scalar(TURN, ANG, 1.0 / TWO_PI, ROUND, ALU.mult, ALU.add))
                link(v.tensor_scalar(TURN, TURN, ROUND, None, ALU.subtract))
                for part in (PI_A, PI_B, PI_C):
                    link(v.scalar_tensor_tensor(ANG, TURN, -part, ANG, ALU.mult, ALU.add))
                link(v.tensor_scalar(SIN[:, f:f + 1, :], ANG, 3.1415925, -3.1415925, ALU.min, ALU.max))
                link(v.tensor_scalar(ANG, SIN[:, f:f + 1, :], -1.0, None, ALU.mult))
                link(v.tensor_tensor(ANG, ANG, SIN[:, f:f + 1, :], ALU.max))
                link(v.tensor_scalar(COS[:, f:f + 1, :], ANG, -1.0, math.pi / 2, ALU.mult, ALU.add))
                dve.sem_inc(freq_dve, 1)
            dve.wait_ge(freq_act, 1 + RET_HEADS + 1)

            def rotate(dst, src, f):
                cos, sin = (a[:, f, :][:, None, :].broadcast_to([P, 2, S]) for a in (COS, SIN))
                v.tensor_tensor(RA, src, cos, ALU.mult)
                return v.tensor_tensor(RB, src, sin, ALU.mult)

            with repeat(dve, 2, (ring, BANKS), (chain, BANKS)) as i:
                for s in range(BANKS):
                    ring.wait_full()
                    ins = rotate(None, halves(ring.bank()), 0)
                    free, count = acc_free[ring.n % BANKS], ring.n // BANKS + 1
                    ring.release(ins)
                    dve.wait_ge(free, count + i)
                    v.tensor_tensor(QK[:, bass.ds(2 * s + i * 8, 1), :], RA[:, 0:1, :], RB[:, 1:2, :], ALU.subtract)
                    link(v.tensor_tensor(QK[:, bass.ds(2 * s + 1 + i * 8, 1), :], RB[:, 0:1, :], RA[:, 1:2, :], ALU.add))
            dve.sem_inc(input_ready, 1)
            ring.n += 8
            for e in range(RET_HEADS):
                dve.wait_ge(scores_ready, e + 1)
                dve.wait_ge(freq_act, 2 + e)
                v.scalar_tensor_tensor(PR[:, 2 * e:2 * e + 2, :], halves(AUX[e]), RET_DK ** -0.5,
                                       DEC[:, 2 * e:2 * e + 2, :], ALU.mult, ALU.mult).then_inc(probs_ready, 1)
            ring.n += 8
            g_uses = ring.n

            def group_norm(e):
                for nt in range(TT):
                    bank = AUX[2 * (e % 2) + nt]
                    dve.wait_ge(y_ready, 2 * e + nt + 1)
                    link(v.bn_stats(BN[:, 0, :], bank[:, :]))
                    if e or nt:
                        dve.wait_ge(yn_ready, 2 * e + nt)
                    link(v.bn_aggr(MV[:, :], BN[:, 0, :]))
                    rooted(RT[:, :], v.tensor_scalar(RT[:, :], MV[:, 1:2], LN_EPS, None, ALU.add))
                    v.tensor_scalar(YN[:, 2 * e + nt, :], bank[:, :], MV[:, 0:1], RT[:, 0:1], ALU.subtract,
                                    ALU.mult).then_inc(yn_ready, 1)

            def gate_heads(e):
                for c in (2 * e, 2 * e + 1):
                    ring.wait_stored(ring.n)
                    ring.n += 1
                    last = v.tensor_tensor(YG[:, 2 * c:2 * c + 2, :], YG[:, 2 * c:2 * c + 2, :],
                                           GS[:, 2 * c:2 * c + 2, :], ALU.mult)
                return last

            for u in range(g_uses - 4, g_uses):
                ring.wait_stored(u)
            group_norm(0)
            group_norm(1)
            gate_heads(0)
            group_norm(2)
            gate_heads(1)
            group_norm(3)
            gate_heads(2)
            gate_heads(3).then_inc(input_ready, 1)

            def add_residual(h):
                for s in range(4):
                    ring.wait_full()
                    ring.release(v.scalar_tensor_tensor(X0[:, 2 * s:2 * s + 2, :], h[:, 2 * s:2 * s + 2, :], ALPHA,
                                                        halves(ring.bank()), ALU.mult, ALU.add))
                for u in range(ring.n - 4, ring.n):
                    ring.wait_stored(u)
                dve.sem_inc(input_ready, 1)

            add_residual(X1)

            def peer(layer):
                centre(X0[:, :, :])
                layer_scale(X0[:, :, :], LN_EPS)
                ring.n += 8
                for tt in range(TT):
                    for half in range(2):
                        ring.wait_full()
                        ring.release(v.tensor_copy(HTM[:, tt, half * 512:(half + 1) * 512], ring.bank()[:, :]))
                score_uses = ring.n
                ring.n += 8
                for u in range(score_uses - 4, ring.n):
                    ring.wait_stored(u)
                dve.wait_ge(rows_loaded, 32 + 16 * layer)
                dve.wait_ge(iota_ready, 1)
                units0, b0 = layer * TT * HEADS, layer * TT * HEADS * 4

                def topk(par, unit, i):
                    at = SCO[:, 2 * unit:2 * unit + 2, :] if i is None else SCO[:, bass.ds(2 * unit + i * 4, 2), :]
                    link_alone(v.tensor_copy(SK, at))
                    for c in range(2):
                        link_alone(v.max(M16[:, c, 0:8], SK[:, c, :]))
                        v.max_index(I16[:, c, 0:8], M16[:, c, 0:8], SK[:, c, :])
                        link_alone(v.match_replace(SL[:, c, :], M16[:, c, 0:8], SK[:, c, :], LOWEST))
                        link_alone(v.max(M16[:, c, 8:16], SL[:, c, :]))
                        link_alone(v.max_index(I16[:, c, 8:16], M16[:, c, 8:16], SL[:, c, :]))
                    link_alone(v.tensor_tensor(CA[:, 0, :].rearrange("p (a b) -> p a b", b=TOPK),
                                               M16[:, 0, :][:, :, None].broadcast_to([P, TOPK, TOPK]),
                                               M16[:, 1, :][:, None, :].broadcast_to([P, TOPK, TOPK]), ALU.add))
                    link_alone(v.max(T16[:, 0:8], CA[:, 0, :]))
                    v.max_index(P16[:, 0:8], T16[:, 0:8], CA[:, 0, :])
                    link_alone(v.match_replace(CB[:, 0, :], T16[:, 0:8], CA[:, 0, :], LOWEST))
                    link_alone(v.max(T16[:, 8:16], CB[:, 0, :]))
                    v.max_index(P16[:, 8:16], T16[:, 8:16], CB[:, 0, :])
                    v.tensor_copy(IF16[:, :, :], I16[:, :, :])
                    link(v.tensor_scalar(NM[:, :], T16[:, 0:1], -1.0, None, ALU.mult))
                    dve.sem_inc(top_ready, 1)
                    v.tensor_scalar(AB[:, 0, :], P16[:, :], 4, None, ALU.logical_shift_right)
                    link(v.tensor_scalar(AB[:, 1, :], P16[:, :], 15, None, ALU.bitwise_and))
                    link(v.tensor_copy(ABF[:, :, :], AB[:, :, :]))
                    oh = OH[:, :, :].rearrange("p c (k a) -> p c k a", a=TOPK)
                    link(v.tensor_tensor(oh, ABF[:, :, :][:, :, :, None].broadcast_to([P, 2, TOPK, TOPK]),
                                         IOTA16[:, None, None, :].broadcast_to([P, 2, TOPK, TOPK]), ALU.is_equal))
                    link(v.tensor_tensor(oh, oh, IF16[:, :, :][:, :, None, :].broadcast_to([P, 2, TOPK, TOPK]), ALU.mult))
                    link(v.tensor_reduce(EI[:, :, :], oh, AX.X, ALU.add))
                    v.scalar_tensor_tensor(EIDX[:, par, :], EI[:, 0, :], float(NKEYS), EI[:, 1, :], ALU.mult,
                                           ALU.add).then_inc(idx_ready, 1)

                LINKS_TOPK = 1 + 2 * 4 + 1 + 3 + 1 + 5

                def gates(par, unit, i):
                    dve.wait_ge(exp_ready, unit if i is None else unit + i * 2)
                    link(v.reciprocal(ES[:, par:par + 1], ES[:, par:par + 1]))
                    link(v.tensor_scalar(GT[:, par, :], EX[:, par, :], ES[:, par:par + 1], None, ALU.mult))

                def batch(tt, q, b, i):
                    for s in range(4):
                        slot = (q % 2) * 4 + s
                        dve.wait_ge(gathered[slot], 16 * (b // 2 + 1) + i * 64)
                        last = v.scalar_tensor_tensor(G[:, slot, 0:D], G[:, slot, 0:D], 1.0, HTM[:, tt, :], ALU.mult,
                                                      ALU.mult, accum_out=HD[:, q % 2, s:s + 1])
                    last.then_inc(dots_ready, 1)
                    dve.wait_ge(gelu_ready, b + 1 + i * 8)
                    v.tensor_tensor(WT[:, q % 2, :], GL[:, q % 2, :], GT[:, q // 4, (q % 4) * 4:(q % 4) * 4 + 4],
                                    ALU.mult).then_inc(weights_ready, 1)

                def output_norm(tt):
                    dve.wait_ge(experts_summed, TT * layer + tt + 1)
                    for c in range(2):
                        last = v.bn_stats(BN[:, c, :], AUX[2 * tt + c][:, :])
                    link(last)
                    link(v.bn_aggr(MV[:, :], BN[:, :, :]))
                    rooted(RT[:, :], v.tensor_scalar(RT[:, :], MV[:, 1:2], LN_EPS, None, ALU.add))
                    for c in range(2):
                        last = v.tensor_scalar(HTM[:, tt, c * 512:(c + 1) * 512], AUX[2 * tt + c][:, :], MV[:, 0:1],
                                               RT[:, 0:1], ALU.subtract, ALU.mult)
                    link(last)
                    link(v.tensor_tensor(HTM[:, tt, :], HTM[:, tt, :], RO[:, 0, :], ALU.mult))
                    v.tensor_tensor(HTM[:, tt, :], HTM[:, tt, :], RO[:, 1, :], ALU.add).then_inc(tokens_normed, 1)

                topk(0, 0, None)
                gates(0, units0 + 1, None)
                for tt in range(TT):
                    loops = HEADS // 2 - tt
                    with repeat(dve, loops, (chain, 2 * (LINKS_TOPK + 2))) as i:
                        for q in range(8):
                            batch(tt, q, b0 + tt * HEADS * 4 + q, i)
                            if q % 4 == 0:
                                unit = tt * HEADS + q // 4 + 1
                                topk(1 - q // 4, unit, i)
                                gates(1 - q // 4, units0 + unit + 1, i)
                    if tt == 0:
                        output_norm(0)
                for q in range(8):
                    batch(1, q, b0 + (TT * HEADS - 2) * 4 + q, 0)
                    if q == 0:
                        topk(1, TT * HEADS - 1, None)
                        gates(1, units0 + TT * HEADS, None)
                output_norm(1)

            peer(0)
            ring.n += 4
            c_uses = ring.n
            ring.n += 4
            for u in range(c_uses, ring.n):
                ring.wait_stored(u)
            rstd(0, 384, LN_EPS)
            link(rms_apply(CN, CC, "q_norm", 0, 3))
            rstd(1, 256, LN_EPS)
            link(rms_apply(CN, CC, "kv_norm", 3, 5, 3))
            dve.sem_inc(input_ready, 1)
            dve.wait_ge(freq_act, 1 + RET_HEADS + 2)

            def rotate_mla(dst, k, src):
                link(rotate(None, src, 1))
                v.tensor_tensor(dst[:, k[0], :], RA[:, 0, :], RB[:, 1, :], ALU.subtract)
                link(v.tensor_tensor(dst[:, k[1], :], RB[:, 0, :], RA[:, 1, :], ALU.add))

            rotate_mla(KR, (0, 1), CC[:, 5:7, :])
            for r in range(2):
                for q in range(4):
                    v.tensor_scalar(KRM[:, 4 * r + q, :], KR[:, r, :], col("quarter", q), None, ALU.mult)
            uq = ring.n
            ring.n += 6 + 4 + 4
            ring.wait_stored(uq + 4)
            ring.wait_stored(uq + 5)
            for half in range(2):
                rotate_mla(QR, (half, 2 + half), QN[:, 8 + half:11 + half:2, :])
            dve.sem_inc(input_ready, 1)

            def probs_max(e):
                dve.wait_ge(mla_scored, e + 1)
                link(v.tensor_reduce(MX[:, e, :], halves(AUX[e % 2]), AX.X, ALU.max))
                v.tensor_scalar(MX[:, e, :], MX[:, e, :], -MLA_SCALE, None, ALU.mult).then_inc(mla_max, 1)

            def probs_norm(e):
                dve.wait_ge(mla_exp, 2 * (e + 1))
                link(v.reciprocal(SU[:, e, :], SU[:, e, :]))
                for qt in range(TT):
                    last = v.tensor_scalar(PS[:, 2 * e + qt, :], PS[:, 2 * e + qt, :], SU[:, e, qt:qt + 1], None, ALU.mult)
                last.then_inc(mla_prob, 1)

            probs_max(0)
            for e in range(MLA_HEADS):
                if e + 1 < MLA_HEADS:
                    probs_max(e + 1)
                probs_norm(e)
            ring.n += 4
            add_residual(X1)
            peer(1)


def _tiles(w, order):
    import numpy as np
    return [w[k * P:(k + 1) * P, n * P:(n + 1) * P] for k, n in order]


def _cm(n_tiles, kt):
    return [(k, n) for n in n_tiles for k in range(kt)]


def _tm(n_tiles, kt):
    return [(k, n) for c in range(0, len(n_tiles), 4) for k in range(kt) for n in n_tiles[c:c + 4]]


def _layout(inputs):
    import numpy as np
    f = lambda name: np.asarray(inputs[name])
    w_in = f("w_in")[0]
    t = []
    seq = range
    t += _tiles(w_in, _cm([n for j in seq(8) for n in (16 + j, 24 + j)], 8))
    t += _tiles(w_in, _cm(seq(32, 40), 8))
    t += _tiles(w_in, _cm(seq(0, 8), 8))
    t += _tiles(w_in, _tm(list(seq(8, 16)), 8))
    t += _tiles(w_in, _cm(seq(40, 64), 8))
    for g in range(4):
        t += _tiles(f("w_pool")[0, g], _cm(seq(2), 2))
    for name in ("w_conv_out", "w_pool_out", "w_sgu_out", "w_out"):
        t += _tiles(f(name)[0], _cm(seq(8), 8))
    t += _tiles(f("w_ffn_in")[0], _cm([n for j in seq(FT) for n in (j, FT + j)], 8))
    t += _tiles(f("w_ffn_out")[0], _cm(seq(8), FT))
    t += _tiles(f("w_ple")[0], _cm(seq(8), 2))
    t += _tiles(f("w_ple_gate")[0], _cm(seq(8), 8))
    ret = f("ret_w_in_2")[0]
    t += _tiles(ret, _cm(seq(0, 16), 8))
    t += _tiles(ret, _tm(list(seq(16, 32)), 8))
    t += _tiles(ret, _cm(seq(32, 48), 8))
    t += _tiles(f("ret_w_out_2")[0], _cm(seq(8), 16))

    def peer(layer):
        a = _tiles(f("peer_w_q_2")[layer], _cm(seq(16), 8))
        keys = f("peer_sub_keys_2")[layer]
        return a + [keys[h, c].T for h in range(HEADS) for c in range(2)]

    t += peer(0)
    m = f("mla_w_in_2")[0]
    r1, r2 = m[:, 640:672], m[:, 672:704]
    m = np.concatenate([m[:, :640]] + [r1] * 4 + [r2] * 4, axis=1)
    t += _tiles(m, _cm(seq(7), 8))
    uq = f("mla_w_uq_2")[0].reshape(384, MLA_HEADS, 192)
    uq = np.concatenate([uq[:, :, :128].reshape(384, -1), uq[:, :, 128:160].reshape(384, -1),
                         uq[:, :, 160:].reshape(384, -1)], axis=1)
    t += _tiles(uq, _cm(seq(12), 3))
    t += [np.zeros((P, P), np.float32)] * 4
    ukv = f("mla_w_ukv_2")[0]
    t += _tiles(ukv, _cm([2 * e for e in seq(8)], 2))
    t += _tiles(ukv, _tm([2 * e + 1 for e in seq(8)], 2))
    t += _tiles(f("mla_w_out_2")[0], _cm(seq(8), 8))
    t += peer(1)
    assert len(t) == BLOCKS * TILES, (len(t), BLOCKS * TILES)
    stream = np.empty((BLOCKS, P, TILES, P), np.float32)
    for i, a in enumerate(t):
        stream[i // TILES, :, i % TILES, :] = a

    def chan(a):
        return np.asarray(a).reshape(-1, P).T

    def freqs(d):
        return np.float32(10000.0) ** (-np.arange(0, d, 2, dtype=np.float32) / np.float32(d))

    cols = {
        "g_mix_pre": chan(f("g_mix_pre")[0]),
        "w_dw": f("w_dw")[0, :, 0, :].reshape(CONV, KT, P).transpose(2, 1, 0).reshape(P, -1),
        "b_dw": chan(f("b_dw")[0]), "g_conv_ln": chan(f("g_conv_ln")[0]), "b_conv_ln": chan(f("b_conv_ln")[0]),
        "s_pool": chan(f("s_pool")[0]), "g_mix_post": chan(f("g_mix_post")[0]),
        "g_ffn_pre": chan(f("g_ffn_pre")[0]), "g_ffn_post": chan(f("g_ffn_post")[0]),
        "gn_g": chan(f("ret_gn_g_2")[0]), "gn_b": chan(f("ret_gn_b_2")[0]),
        "q_norm": chan(f("mla_q_norm_2")[0]), "kv_norm": chan(f("mla_kv_norm_2")[0]),
        "ln_g0": chan(f("ln_mix_g_2")[0]), "ln_b0": chan(f("ln_mix_b_2")[0]),
        "ln_g1": chan(f("ln_mix_g_2")[1]), "ln_b1": chan(f("ln_mix_b_2")[1]),
        "freq_ret": freqs(RET_DK)[:, None], "freq_mla": np.tile(freqs(64), 4)[:, None],
        "quarter": (np.arange(P)[:, None] // 32 == np.arange(4)[None, :]).astype(np.float32),
    }
    cols = np.concatenate([cols[name] for name, _ in _COLS], axis=1)
    rows = np.stack([f("g_sgu_v")[0], f("b_sgu_v")[0], f("b_sgu_s")[0].reshape(-1), f("ln_ffn_g_2")[0],
                     f("ln_ffn_b_2")[0], f("ln_ffn_g_2")[1], f("ln_ffn_b_2")[1]])

    def cm(a):
        return a.T.reshape(-1, P, S).transpose(1, 0, 2)

    t1 = np.arange(1, S + 1, dtype=np.float32)
    return {
        "stream": stream, "cols": cols, "rows": rows, "x_cm": cm(f("x")[0]), "p_cm": cm(f("p")[0, 0]),
        "sgu_wt": f("w_sgu_s")[0].transpose(2, 0, 1),
        "rcnt": np.stack([1.0 / np.minimum(t1, np.float32(w)) for w in WINDOWS]).astype(np.float32),
        "positions": f("positions_2")[0].astype(np.int32), "decay": f("ret_log1m_decay_2")[0].reshape(-1),
        "uv0": np.concatenate([f("peer_u_2")[0], f("peer_v_2")[0]], axis=1),
        "uv1": np.concatenate([f("peer_u_2")[1], f("peer_v_2")[1]], axis=1),
    }


def kernel(**inputs):
    import numpy as np
    import concourse.bacc as bacc
    from concourse.bass_utils import run_bass_kernel_spmd as run

    nc = bacc.Bacc("TRN2", target_bir_lowering=False, num_devices=1)
    arrays = {k: np.ascontiguousarray(a) for k, a in _layout(inputs).items()}
    ap = {k: nc.dram_tensor(k, a.shape, mybir.dt.from_np(a.dtype), kind="ExternalInput").ap() for k, a in arrays.items()}
    out = nc.dram_tensor("out", (1, S, D), FP32, kind="ExternalOutput").ap()
    build(nc, ap["stream"], ap["cols"], ap["rows"], ap["x_cm"], ap["p_cm"], ap["sgu_wt"], ap["rcnt"],
          ap["positions"], ap["decay"], ap["uv0"], ap["uv1"], out)
    return run(nc, [arrays], core_ids=[0]).results[0]["out"]
```

```python
import math
from contextlib import ExitStack, contextmanager

import concourse.bass as bass
from concourse import mybir

FP32 = mybir.dt.float32
I32 = mybir.dt.int32
U32 = mybir.dt.uint32
ALU = mybir.AluOpType
ACT = mybir.ActivationFunctionType
AX = mybir.AxisListType

P = 128
D = 1024
S = 256
KT = D // P
TT = S // P
EPS = 1e-6
LN_EPS = 1e-5
CONV = 31
PAD = CONV - 1
ZPAD = 16
WINDOWS = (2, 4, 8, 16)
D_FF = 2816
FT = D_FF // P
ALPHA = 4.0 ** 0.25
RET_HEADS, RET_DK, RET_DV = 4, 256, 512
MLA_HEADS = 8
MLA_SCALE = (128 + 64) ** -0.5
HEADS, TOPK, NKEYS = 8, 16, 128
EXPERTS = NKEYS * NKEYS
LOWEST = -3.0e38
RING = 8
GROUP = 2
PARTS = RING // GROUP
GROUPS = TOPK // GROUP
AHEAD = 3
TWO_PI = 2.0 * math.pi
PI_A = 6.28125
PI_B = 0.0019350051879882812
PI_C = TWO_PI - PI_A - PI_B
ROUND = 1.5 * 2.0 ** 23

TILES = 16
SLOTS = 4
BANKS = 4

STREAM = [("conv", 8), ("pool", 4), ("u", 4), ("v", 4), ("gates", 12), ("w_pool", 1), ("br_conv", 4),
          ("br_pool", 4), ("br_sgu", 4), ("w_out", 4), ("ffn_in", 22), ("ffn_out", 11), ("ple", 1),
          ("ple_gate", 4), ("ret_qk", 8), ("ret_v", 8), ("ret_g", 8), ("ret_out", 8), ("peer_q0", 8),
          ("mla_in_uq", 6), ("mla_k", 1), ("mla_v", 1), ("mla_out", 4), ("peer_q1", 8)]
BLOCKS = sum(n for _, n in STREAM)

_COLS = [("g_mix_pre", 8), ("w_dw", 8 * CONV), ("b_dw", 8), ("g_conv_ln", 8), ("b_conv_ln", 8), ("s_pool", 8),
         ("g_mix_post", 8), ("g_ffn_pre", 8), ("g_ffn_post", 8), ("gn_g", 16), ("gn_b", 16), ("q_norm", 3),
         ("kv_norm", 2), ("ln_g0", 8), ("ln_b0", 8), ("ln_g1", 8), ("ln_b1", 8), ("freq_ret", 1),
         ("freq_mla", 1), ("quarter", 4)]
COL, _n = {}, 0
for _name, _w in _COLS:
    COL[_name] = _n
    _n += _w
NCOL = _n


class Chain:

    def __init__(self, eng, sem, plain=None):
        self.eng, self.sem, self.n, self.i, self.per, self.plain = eng, sem, 0, None, 0, plain

    def enter(self, i, per):
        self.i, self.per, self.at = i, per, self.n

    def leave(self, times):
        assert self.n - self.at == self.per, (self.n - self.at, self.per)
        self.n, self.i = self.at + self.per * times, None

    def link(self, ins):
        self.n += 1
        ins.then_inc(self.sem, 1)
        self.eng.wait_ge(self.sem, self.n if self.i is None else self.n + self.i * self.per)

    def step(self, ins):
        self.n += 1
        ins.then_inc(self.sem, 1)

    def wait_back(self, back):
        n = self.n - back
        self.eng.wait_ge(self.sem, n if self.i is None else n + self.i * self.per)

    def link_alone(self, ins):
        self.link(ins)
        if self.i is not None:
            self.eng.sem_inc(self.plain, 1)


class Turns:

    def __init__(self, eng, full, free, banks, plain=None):
        self.plain = plain
        self.eng, self.full, self.free, self.banks, self.n, self.i = eng, full, free, banks, 0, None

    def enter(self, i, per):
        self.i, self.at, self.per = i, self.n, per

    def leave(self, times):
        assert self.n - self.at == self.per == BANKS
        self.n, self.i = self.at + BANKS * times, None

    def wait(self, sem, count):
        if self.i is None:
            if count > 0:
                self.eng.wait_ge(sem, count)
        else:
            self.eng.wait_ge(sem, count + self.i)

    def bank(self):
        return self.banks[self.n % BANKS]

    def wait_full(self):
        self.wait(self.full[self.n % BANKS], self.n // BANKS + 1)

    def wait_full_alone(self):
        self.wait_full()
        if self.i is not None:
            self.eng.sem_inc(self.plain, 1)

    def wait_free(self):
        self.wait(self.free[self.n % BANKS], self.n // BANKS)

    def wait_stored(self, use):
        self.wait(self.free[use % BANKS], use // BANKS + 1)

    def release(self, ins):
        ins.then_inc(self.free[self.n % BANKS], 1)
        self.n += 1

    def filled(self, ins):
        ins.then_inc(self.full[self.n % BANKS], 1)
        self.n += 1


@contextmanager
def repeat(eng, times, *counters):
    with eng.Fori(0, times) as i:
        for c, per in counters:
            c.enter(i, per)
        yield i
    for c, _ in counters:
        c.leave(times)


def build(nc, stream, keys, cols, rows, x_cm, p_cm, sgu_wt, rcnt_in, positions, decay, uv0, uv1, out):
    ctx = ExitStack()
    with ctx:
        def sb(name, shape, dt=FP32):
            return ctx.enter_context(nc.sbuf_tensor(name, shape, dt))

        def sem(name):
            return ctx.enter_context(nc.semaphore(name))

        WR = sb("w_ring", [P, SLOTS, TILES, P])
        CO = sb("channel_vectors", [P, NCOL])
        RO = sb("row_vectors", [P, 3, D])
        IDENT = sb("ident", [P, P])
        ALPHA_I = sb("alpha_ident", [P, P])
        ZERO = sb("zero_square", [P, P])
        ONES = sb("ones", [P, P])
        X0 = sb("x0", [P, KT, S])
        X1 = sb("x1", [P, KT, S])
        SC = sb("scratch", [P, KT, S])
        MU = sb("mu", [P, S])
        RS = sb("rstd", [P, S])
        AR = sb("arena", [P, 120 * S])

        def region(tile, n, t=S, dt=None):
            a = AR[:, int(tile * S):int(tile * S) + n * t].rearrange("p (k t) -> p k t", t=t)
            return a if dt is None else a.bitcast(dt)

        PADH = region(0, KT, PAD + S)
        CV = region(9, KT)
        PADZ = region(17, KT, ZPAD + S)
        PA = region(26, 2, ZPAD + S)
        PB = region(28.5, 2, ZPAD + S)
        POOLED = region(31, KT)
        POOLMIX = region(39, KT)
        U = region(47, KT)
        VT = region(55, TT, D)
        AIN = region(63, KT)
        GATES = region(71, 3 * KT)
        MERGED = region(95, KT)
        RC = region(103, 4)
        SG = region(107, 4)
        WS = AR[:, 111 * S:115 * S].rearrange("p (h i) -> p h i", i=P)
        PT = region(115, 2)
        F = region(0, FT)
        MO = region(31, KT)
        PL = region(39, KT)
        QK = region(0, 16)
        V = region(16, TT, 2048)
        GS = region(32, 16)
        DEC = region(48, 8)
        PR = region(56, 8)
        YN = region(64, 8, RET_DV)
        YG = region(80, 16)
        COS, SIN = region(96, 2), region(98, 2)
        RA, RB = region(100, 2), region(102, 2)
        DIFF = region(104, 2)
        DNEG = region(106, 2)
        POSF = region(108, 1)
        ANG = region(109, 1)
        TURN = region(110, 1)
        POSI = region(111, 1, dt=I32)
        DIFI = region(112, 2, dt=I32)
        DC = sb("decay_rates", [P, 5, 2 * RET_HEADS])
        CC = region(0, 7)
        CN = region(7, 5)
        KR = region(12, 2)
        QN = region(14, 12)
        QR = region(82, 4)
        KN = region(26, KT)
        VM = region(34, TT, D)
        PS = region(42, 2 * MLA_HEADS)
        PTT = region(58, 2 * MLA_HEADS)
        OM = region(74, MLA_HEADS)
        KRM = region(86, 8)
        G = region(0, RING, 2 * D)
        SCO = region(64, 2 * HEADS * TT, NKEYS)
        QT = region(80, 16)
        HTM = region(101, TT, D)
        DG = region(109, RING, P)
        SK = region(113, 2, NKEYS)
        SL = region(114, 2, NKEYS)
        CA = region(115, 1)
        CB = region(116, 1)
        OH = region(117, 2)
        KEYS = X1[:, :, :].rearrange("p k t -> p (k t)").rearrange("p (j n) -> p j n", n=NKEYS)
        IOTA16 = sb("iota16", [P, TOPK])
        IOTAI = sb("iota16_int", [P, TOPK], I32)
        M16 = sb("top_per_side", [P, 2, TOPK])
        I16 = sb("index_per_side", [P, 2, TOPK], U32)
        IF16 = sb("index_per_side_float", [P, 2, TOPK])
        T16 = sb("top_pairs", [P, TOPK])
        P16 = sb("place_of_pairs", [P, TOPK], U32)
        AB = sb("place_halves", [P, 2, TOPK], U32)
        ABF = sb("place_halves_float", [P, 2, TOPK])
        EI = sb("expert_halves", [P, 2, TOPK])
        EIDX = sb("expert_index", [P, 2, TOPK], I32)
        NM = sb("minus_top", [P, 1])
        EX = sb("exp_top", [P, 2, TOPK])
        ES = sb("exp_sum", [P, 2])
        GT = sb("gate", [P, 2, TOPK])
        HD = sb("dots", [P, 2, GROUP])
        GL = sb("gelu_dots", [P, 2, GROUP])
        WT = sb("expert_weights", [P, 2, GROUP])
        BN = sb("bn_parts", [P, 2, 6])
        MV = sb("mean_var", [P, 2])
        RT = sb("rstd_tokens", [P, 1])
        MX = sb("score_max", [P, MLA_HEADS, 2])
        SU = sb("prob_sum", [P, MLA_HEADS, 2])

        def psum(name):
            return ctx.enter_context(nc.psum_tensor(name, [P, 512], FP32))

        ACC = [psum(f"acc{i}") for i in range(BANKS)]
        AUX = [psum(f"aux{i}") for i in range(4)]

        def halves(bank):
            return bank[:, :].rearrange("p (a t) -> p a t", a=2)

        def col(name, k=0, n=1):
            return CO[:, COL[name] + k:COL[name] + k + n]

        w_full = [sem(f"w_full{i}") for i in range(SLOTS)]
        w_free = [sem(f"w_free{i}") for i in range(SLOTS)]
        acc_full = [sem(f"acc_full{i}") for i in range(BANKS)]
        acc_free = [sem(f"acc_free{i}") for i in range(BANKS)]
        act_chain, dve_chain, pool_chain = sem("act_chain"), sem("dve_chain"), sem("pool_chain")
        x_loaded, cols_loaded, rows_loaded = sem("x_loaded"), sem("cols_loaded"), sem("rows_loaded")
        small_loaded, sgu_w_loaded, pos_loaded = sem("small_loaded"), sem("sgu_w_loaded"), sem("pos_loaded")
        p_loaded = sem("p_loaded")
        ones_ready, ident_ready, pads_ready = sem("ones_ready"), sem("ident_ready"), sem("pads_ready")
        squares_ready = sem("squares_ready")
        sums_ready = sem("sums_ready")
        var_ready = sem("var_ready")
        root_ready = sem("root_ready")
        centred = sem("centred")
        input_ready = sem("input_ready")
        input_ready_act = sem("input_ready_act")
        scaled = sem("scaled")
        gate_half = sem("gate_half")
        pooled_ready = sem("pooled_ready")
        sgu_w_ready = sem("sgu_w_ready")
        mix_ready = sem("mix_ready")
        ple_gated = sem("ple_gated")
        freq_act, freq_dve = sem("freq_act"), sem("freq_dve")
        iota_ready = sem("iota_ready")
        scores_ready, probs_ready = sem("scores_ready"), sem("probs_ready")
        y_ready, yn_ready = sem("y_ready"), sem("yn_ready")
        mla_scored, mla_max, mla_exp, mla_prob = sem("mla_scored"), sem("mla_max"), sem("mla_exp"), sem("mla_prob")
        mla_turned, mla_probs_cm = sem("mla_turned"), sem("mla_probs_cm")
        waits_passed = sem("waits_passed")
        keys_loaded = sem("keys_loaded")
        head_scored = sem("head_scored")
        idx_ready = sem("idx_ready")
        top_ready = sem("top_ready")
        exp_ready = sem("exp_ready")
        gathered = [sem(f"gathered{i}") for i in range(RING)]
        group_free = sem("group_free")
        dots_ready, gelu_ready = sem("dots_ready"), sem("gelu_ready")
        weights_ready, diag_ready = sem("weights_ready"), sem("diag_ready")
        experts_summed = sem("experts_summed")
        tokens_normed = sem("tokens_normed")
        stored = sem("stored")

        block = ctx.enter_context(nc.Block())

        @block.sync
        def _(sp):
            sp.dma_start(X0[:, :, :], x_cm).then_inc(x_loaded, 16)
            for s in range(SLOTS):
                sp.dma_start(WR[:, s, :, :], stream[s]).then_inc(w_full[s], 16)
            groups = BLOCKS // SLOTS

            def send(g, s):
                sp.wait_ge(w_free[s], g + 1 if s == SLOTS - 1 else g)
                sp.dma_start(WR[:, s, :, :], stream[bass.ds(SLOTS * g + s, 1)].rearrange("o p a b -> p (o a) b")
                             if not isinstance(g, int) else stream[SLOTS * g + s]).then_inc(w_full[s], 16)

            with sp.Fori(1, groups) as g:
                for s in range(SLOTS):
                    send(g, s)
            for s in range(BLOCKS % SLOTS):
                send(groups, s)
            for tt in range(TT):
                sp.wait_ge(tokens_normed, TT + tt + 1)
                sp.dma_start(out[0, tt * P:(tt + 1) * P, :], HTM[:, tt, :]).then_inc(stored, 16)
            sp.wait_ge(stored, 16 * TT)

        @block.tensor
        def _(pe):
            t = [0]
            ring = Turns(pe, acc_full, acc_free, ACC)
            n = dict(squares=0, inp=0, inp_act=0)

            def tile(i, width=1):
                b, at = divmod(t[0], TILES)
                first = at == 0
                if first:
                    if i is None:
                        pe.wait_ge(w_full[b % SLOTS], 16 * (b // SLOTS + 1))
                    else:
                        pe.wait_ge(w_full[b % SLOTS], 16 * (b // SLOTS + 1) + i * 16)
                t[0] += width
                w = WR[:, b % SLOTS, at:at + width, :]
                return w, ((b - 1) % SLOTS if first else None)

            def entered(ins, slot):
                if slot is not None:
                    ins.then_inc(w_free[slot], 1)

            def output_tile(x, kt, half, i=None, ready=None):
                for k in range(kt):
                    if ready and k % (kt // 2) == 0:
                        ready()
                    w, slot = tile(i)
                    last = nc.tensor.matmul(ring.bank()[:, half * S:(half + 1) * S], w[:, 0, :], x[:, k, :],
                                            start=(k == 0), stop=(k == kt - 1))
                    entered(last, slot)
                return last

            def pairs(x, kt, tiles, halves_ready=None, i=None):
                for o in range(tiles):
                    if o % 2 == 0:
                        ring.wait_free()
                    last = output_tile(x, kt, o % 2, i, halves_ready if o == 0 else None)
                    if o % 2 or o == tiles - 1:
                        ring.filled(last)

            def token_major(x, kt, chunks, i=None):
                for _ in range(chunks):
                    ring.wait_free()
                    at, b0 = ring.n, ring.bank()
                    ring.n += 1
                    ring.wait_free()
                    b1 = ring.bank()
                    ring.n = at
                    for k in range(kt):
                        w, slot = tile(i, 4)
                        w = w.rearrange("p a b -> p (a b)")
                        for tt, bank in enumerate((b0, b1)):
                            last = nc.tensor.matmul(bank[:, :], x[:, k, tt * P:(tt + 1) * P], w,
                                                    start=(k == 0), stop=(k == kt - 1))
                            if tt == 0:
                                entered(last, slot)
                                if k == kt - 1:
                                    ring.filled(last)
                    ring.filled(last)

            def loop(fn, times, *args):
                t0 = t[0]
                with repeat(pe, times, (ring, BANKS)) as i:
                    fn(*args, i=i)
                assert t[0] - t0 == SLOTS * TILES
                t[0] = t0 + SLOTS * TILES * times

            def need_input():
                n["inp"] += 1
                pe.wait_ge(input_ready, n["inp"])

            def need_input_act():
                n["inp_act"] += 1
                pe.wait_ge(input_ready_act, n["inp_act"])

            def stored_by_evacuation(uses=BANKS):
                for u in range(ring.n - uses, ring.n):
                    ring.wait_stored(u)

            def channel_sums(x, kt, half=0, per=None):
                for k in range(kt):
                    if per and k % per == 0:
                        n["squares"] += 1
                        pe.wait_ge(squares_ready, n["squares"])
                    last = nc.tensor.matmul(AUX[3 - half][:, 0:S], ONES[:, :], x[:, k, :],
                                            start=(k == 0), stop=(k == kt - 1))
                last.then_inc(sums_ready, 1)

            def square_sums(x=SC, kt=KT, half=0, per=None):
                channel_sums(x, kt, half, per or kt)

            def pairs_and_sums(x, kt, src, squares):
                first = ring.n

                def add_sums(s):
                    if squares:
                        n["squares"] += 1
                        pe.wait_ge(squares_ready, n["squares"])
                    else:
                        ring.wait_stored(first + s)
                    for k in (2 * s, 2 * s + 1):
                        last = nc.tensor.matmul(AUX[3][:, 0:S], ONES[:, :], src[:, k, :], start=(k == 0),
                                                stop=(k == KT - 1))
                    return last

                for s in range(KT // 2):
                    pairs(x, kt, 2)
                    if s:
                        add_sums(s - 1)
                add_sums(KT // 2 - 1).then_inc(sums_ready, 1)

            pe.wait_ge(ones_ready, 1)
            square_sums()
            pairs(X1, KT, 8, need_input)
            pairs(X1, KT, 8)
            pairs(X1, KT, 8)
            pairs(X1, KT, 8)
            token_major(X1, KT, 2)
            need_input()
            channel_sums(CV, KT)
            pairs(X1, KT, 8)
            square_sums(half=1, per=KT // 2)
            loop(pairs, 2, X1, KT, 8)
            pe.wait_ge(pooled_ready, 1)
            for g in range(4):
                pairs(POOLED[:, 2 * g:2 * g + 2, :], 2, 2)
            need_input()
            pe.wait_ge(sgu_w_ready, 1)
            for h in range(8):
                for b in range(TT):
                    c = (h % 2) * S + b * P
                    last = nc.tensor.matmul(AUX[h // 2][:, c:c + P], VT[:, b, h * P:(h + 1) * P], WS[:, h, :],
                                            start=True, stop=True)
                if h % 2:
                    last.then_inc(mix_ready, 1)
            pairs(CV, KT, 8, need_input_act)
            pairs(POOLMIX, KT, 8)
            need_input()
            pairs(AIN, KT, 8)
            need_input()
            pairs_and_sums(MERGED, KT, SC, True)
            square_sums(per=2)
            loop(pairs, 5, X1, KT, 8, need_input)
            pairs(X1, KT, 4)
            stored_by_evacuation()
            pairs_and_sums(F, FT, SC, True)
            pe.wait_ge(p_loaded, 16)
            pairs(PT, 2, 8)
            need_input()
            pairs(X0, KT, 8)
            need_input()
            loop(pairs, 2, X1, KT, 8)
            loop(token_major, 2, X1, KT, 2)
            need_input()
            for e in range(RET_HEADS):
                for mt in range(TT):
                    for d in range(2):
                        last = nc.tensor.matmul(AUX[e][:, mt * S:(mt + 1) * S],
                                                QK[:, 8 + 2 * e + d, mt * P:(mt + 1) * P], QK[:, 2 * e + d, :],
                                                start=(d == 0), stop=(d == 1))
                last.then_inc(scores_ready, 1)
            stored_by_evacuation()
            loop(pairs, 2, X1, KT, 8)
            pe.wait_ge(probs_ready, RET_HEADS)

            def weigh(e):
                if e >= 2:
                    pe.wait_ge(yn_ready, 2 * (e - 1))
                for nt in range(TT):
                    for mt in range(TT):
                        last = nc.tensor.matmul(AUX[2 * (e % 2) + nt][:, :],
                                                PR[:, 2 * e + mt, nt * P:(nt + 1) * P],
                                                V[:, mt, e * RET_DV:(e + 1) * RET_DV], start=(mt == 0), stop=(mt == 1))
                    last.then_inc(y_ready, 1)

            def turn(e):
                pe.wait_ge(yn_ready, 2 * (e + 1))
                for c in range(4):
                    if c % 2 == 0:
                        ring.wait_free()
                    for nt in range(TT):
                        at = (c % 2) * S + nt * P
                        last = nc.tensor.transpose(ring.bank()[:, at:at + P], YN[:, 2 * e + nt, c * P:(c + 1) * P],
                                                   IDENT[:, :])
                    if c % 2:
                        ring.filled(last)

            weigh(0)
            weigh(1)
            turn(0)
            weigh(2)
            turn(1)
            weigh(3)
            turn(2)
            turn(3)
            need_input()
            pairs_and_sums(YG, 16, X0, False)
            square_sums(half=1, per=KT // 2)

            def key_scores(head):
                ring.wait_free()
                for tt in range(TT):
                    for c in range(2):
                        at = (2 * tt + c) * NKEYS
                        last = nc.tensor.matmul(ring.bank()[:, at:at + NKEYS],
                                                QT[:, 2 * head + c, tt * P:(tt + 1) * P],
                                                KEYS[:, 2 * head + c, :], start=True, stop=True)
                ring.filled(last)

            def peer(layer):
                queries = ring.n
                pairs(X0, KT, 2, need_input_act)
                for tt in range(TT):
                    for half in range(2):
                        ring.wait_free()
                        for k in range(4):
                            last = nc.tensor.transpose(ring.bank()[:, k * P:(k + 1) * P],
                                                       X0[:, 4 * half + k, tt * P:(tt + 1) * P], IDENT[:, :])
                        ring.filled(last)
                pe.wait_ge(keys_loaded, 16 * (layer + 1))
                ring.wait_stored(queries)
                key_scores(0)
                for u in range(queries + 1, queries + 1 + 2 * TT):
                    ring.wait_stored(u)
                for tt in range(TT):
                    for c in range(2):
                        last = nc.tensor.matmul(AUX[2 * tt + c][:, :], ALPHA_I[:, :], HTM[:, tt, c * 512:(c + 1) * 512],
                                                start=True, stop=False)
                        last.then_inc(group_free, PARTS // (2 * TT))
                for head in range(1, AHEAD):
                    before = ring.n
                    pairs(X0, KT, 2)
                    if head > 1:
                        ring.wait_stored(before - 1)
                        key_scores(head - 1)

            def weigh_group(tt, q, count):
                pe.wait_ge(diag_ready, count)
                for s in range(GROUP):
                    slot = (q % PARTS) * GROUP + s
                    for c in range(2):
                        last = nc.tensor.matmul(AUX[2 * tt + c][:, :], DG[:, slot, :],
                                                G[:, slot, D + c * 512:D + (c + 1) * 512], start=False, stop=False)
                last.then_inc(group_free, 1)

            def later_heads(q):
                head, half = q // 2 + AHEAD, q % 2
                if head < HEADS:
                    if half == 0:
                        ring.wait_free()
                    last = output_tile(X0, KT, half)
                    if half:
                        ring.filled(last)
                if half == (1 if head < HEADS else 0) and head <= HEADS:
                    ring.wait_stored(ring.n - 3 if head < HEADS else ring.n - 2)
                    key_scores(head - 1)

            def experts(layer):
                base = layer * TT * HEADS * GROUPS
                for q in range(2 * GROUPS):
                    weigh_group(0, q, base + q + 1)
                    later_heads(q)
                for tt in range(TT):
                    first = 1 if tt == 0 else 0
                    b = base + tt * HEADS * GROUPS + first * 2 * GROUPS
                    with pe.Fori(0, HEADS // 2 - first) as i:
                        for q in range(2 * GROUPS):
                            weigh_group(tt, q, b + q + 1 + i * 2 * GROUPS)
                    for c in range(2):
                        last = nc.tensor.matmul(AUX[2 * tt + c][:, :], ZERO[:, :], HTM[:, tt, c * 512:(c + 1) * 512],
                                                start=False, stop=True)
                    last.then_inc(experts_summed, 1)

            peer(0)
            experts(0)
            pe.wait_ge(tokens_normed, TT)
            for s in range(4):
                ring.wait_free()
                for k in range(2):
                    for tt in range(TT):
                        at = k * S + tt * P
                        last = nc.tensor.transpose(ring.bank()[:, at:at + P], HTM[:, tt, (2 * s + k) * P:(2 * s + k + 1) * P],
                                                   IDENT[:, :])
                ring.filled(last)
            stored_by_evacuation()
            pairs(X1, KT, 7)
            square_sums(kt=3)
            square_sums(SC[:, 3:5, :], kt=2, half=1)
            need_input()
            pairs(CN, 3, 12)
            t[0] += 4
            pairs(CN[:, 3:5, :], 2, 8)
            token_major(CN[:, 3:5, :], 2, 2)
            need_input()
            stored_by_evacuation(8)

            def score(e):
                if e >= 2:
                    pe.wait_ge(mla_exp, 2 * (e - 1))
                for qt in range(TT):
                    o = AUX[e % 2][:, qt * S:(qt + 1) * S]
                    nc.tensor.matmul(o, QN[:, e, qt * P:(qt + 1) * P], KN[:, e, :], start=True, stop=False)
                    nc.tensor.matmul(o, QR[:, e // 4, qt * P:(qt + 1) * P], KRM[:, e % 4, :], start=False, stop=False)
                    last = nc.tensor.matmul(o, QR[:, 2 + e // 4, qt * P:(qt + 1) * P], KRM[:, 4 + e % 4, :],
                                            start=False, stop=True)
                last.then_inc(mla_scored, 1)

            def turn_probs(e):
                pe.wait_ge(mla_prob, e + 1)
                if e >= 2:
                    pe.wait_ge(mla_probs_cm, e - 1)
                for kt in range(TT):
                    for qt in range(TT):
                        at = kt * S + qt * P
                        last = nc.tensor.transpose(AUX[2 + e % 2][:, at:at + P], PS[:, 2 * e + qt, kt * P:(kt + 1) * P],
                                                   IDENT[:, :])
                last.then_inc(mla_turned, 1)

            def weigh_values(e):
                pe.wait_ge(mla_probs_cm, e + 1)
                if e % 2 == 0:
                    ring.wait_free()
                for kt in range(TT):
                    last = nc.tensor.matmul(ring.bank()[:, (e % 2) * S:(e % 2 + 1) * S], VM[:, kt, e * P:(e + 1) * P],
                                            PTT[:, 2 * e + kt, :], start=(kt == 0), stop=(kt == 1))
                if e % 2:
                    ring.filled(last)

            for e in range(MLA_HEADS + 2):
                if e < MLA_HEADS:
                    score(e)
                if 0 <= e - 1 < MLA_HEADS:
                    turn_probs(e - 1)
                if e >= 2:
                    weigh_values(e - 2)
            stored_by_evacuation()
            pairs_and_sums(OM, MLA_HEADS, X0, False)
            square_sums(half=1, per=KT // 2)
            peer(1)
            experts(1)
            assert t[0] == BLOCKS * TILES, (t[0], BLOCKS * TILES)

        @block.gpsimd
        def _(pool):
            chain = Chain(pool, pool_chain)
            link = chain.link
            nc.gpsimd.memset(ONES[:, :], 1.0).then_inc(ones_ready, 1)
            nc.gpsimd.memset(PADH[:, :, 0:PAD], 0.0)
            nc.gpsimd.memset(PADZ[:, :, 0:ZPAD], 0.0).then_inc(pads_ready, 1)
            link(nc.gpsimd.memset(IDENT[:, :], 1.0))
            link(nc.gpsimd.affine_select(out=IDENT[:, :], in_=IDENT[:, :], pattern=[[-1, P]],
                                         compare_op=ALU.is_equal, fill=0.0, base=0, channel_multiplier=1))
            nc.gpsimd.memset(ZERO[:, :], 0.0)
            link(nc.gpsimd.memset(ALPHA_I[:, :], ALPHA))
            nc.gpsimd.affine_select(out=ALPHA_I[:, :], in_=ALPHA_I[:, :], pattern=[[-1, P]],
                                    compare_op=ALU.is_equal, fill=0.0, base=0,
                                    channel_multiplier=1).then_inc(ident_ready, 1)
            link(nc.gpsimd.iota(IOTAI[:, :], pattern=[[1, TOPK]], base=0, channel_multiplier=0))
            link(nc.gpsimd.tensor_copy(IOTA16[:, :], IOTAI[:, :]))
            pool.sem_inc(iota_ready, 1)
            pool.wait_ge(sgu_w_loaded, 16)
            link(nc.gpsimd.memset(WS[P // 2:P, :, 0:P // 2], 0.0))
            pool.sem_inc(sgu_w_ready, 1)
            pool.wait_ge(small_loaded, 16)
            for u in range(8, 12):
                pool.wait_ge(acc_free[u % BANKS], u // BANKS + 1)
            for g in range(len(WINDOWS)):
                src, lo = PADZ[:, 2 * g:2 * g + 2, :], 0
                for n in range(g + 1):
                    dst, step = (PA, PB)[n % 2], 2 ** n
                    lo += step
                    link(nc.gpsimd.tensor_tensor(dst[:, :, lo:ZPAD + S], src[:, :, lo:ZPAD + S],
                                                 src[:, :, lo - step:ZPAD + S - step], ALU.add))
                    src = dst
                link(nc.gpsimd.tensor_tensor(POOLED[:, 2 * g:2 * g + 2, :], src[:, :, ZPAD:ZPAD + S],
                                             RC[:, g:g + 1, :].broadcast_to([P, 2, S]), ALU.mult))
                last = nc.gpsimd.tensor_tensor(POOLED[:, 2 * g:2 * g + 2, :], POOLED[:, 2 * g:2 * g + 2, :],
                                               PADZ[:, 2 * g:2 * g + 2, ZPAD:ZPAD + S], ALU.subtract)
                link(last) if g < 3 else last.then_inc(pooled_ready, 1)
            pool.wait_ge(input_ready, 10)
            nc.gpsimd.iota(DIFI, pattern=[[-P, 2], [1, S]], base=0, channel_multiplier=-1).then_inc(iota_ready, 1)
            for layer in range(2):
                uv = (uv0, uv1)[layer]
                for tt in range(TT):
                    base = (layer * TT + tt) * HEADS * GROUPS
                    with pool.Fori(0, HEADS // 2) as i:
                        for q in range(2 * GROUPS):
                            pool.wait_ge(group_free, PARTS * layer + base + q + 1 + i * 2 * GROUPS)
                            if q % GROUPS == 0:
                                unit = base // GROUPS + q // GROUPS
                                pool.wait_ge(idx_ready, unit + 1 + i * 2)
                            pool.sem_inc(waits_passed, 1)
                            for s in range(GROUP):
                                slot = (q % PARTS) * GROUP + s
                                k = (q % GROUPS) * GROUP + s
                                pool.indirect_dma_start(
                                    G[:, slot, :], None, uv,
                                    bass.IndirectOffsetOnAxis(ap=EIDX[:, q // GROUPS, k:k + 1], axis=0),
                                ).then_inc(gathered[slot], 16)

        @block.scalar
        def _(act):
            chain = Chain(act, act_chain)
            link = chain.link
            ring = Turns(act, acc_full, acc_free, ACC, waits_passed)
            n = dict(centred=0, scaled=0, roots=0)
            act.dma_start(CO[:, :], cols).then_inc(cols_loaded, 16)
            act.dma_start(RO[:, 0:3, :], rows[0:3].partition_broadcast(P)).then_inc(rows_loaded, 16)
            act.dma_start(RC, rcnt_in.partition_broadcast(P)).then_inc(small_loaded, 16)
            act.dma_start(WS, sgu_wt).then_inc(sgu_w_loaded, 16)
            act.dma_start(PT, p_cm).then_inc(p_loaded, 16)

            def evacuate(func, dst, scale=1.0):
                ring.wait_full_alone()
                ring.release(nc.scalar.activation(dst, halves(ring.bank()), func, scale=scale))

            def evacuate_tm(func, dst):
                ring.wait_full_alone()
                ring.release(nc.scalar.activation(dst, ring.bank()[:, :], func))

            def root(x, times=1):
                for _ in range(times):
                    n["roots"] += 1
                    act.wait_ge(var_ready, n["roots"])
                    nc.scalar.activation(x[:, :], x[:, :], ACT.Sqrt).then_inc(root_ready, 1)

            def square(dst, src):
                n["centred"] += 1
                act.wait_ge(centred, n["centred"])
                nc.scalar.activation(dst, src, ACT.Square).then_inc(squares_ready, 1)

            def square_halves(src):
                for k in (0, KT // 2):
                    square(SC[:, k:k + KT // 2, :], src[:, k:k + KT // 2, :])

            def gain_bias(dst, src, g, b, func=ACT.Identity):
                for half in range(2):
                    n["scaled"] += 1
                    act.wait_ge(scaled, n["scaled"])
                    for k in range(half * KT // 2, (half + 1) * KT // 2):
                        last = nc.scalar.activation(dst[:, k, :], src[:, k, :], func, bias=col(b, k), scale=col(g, k))
                    last.then_inc(input_ready_act, 1)

            act.wait_ge(x_loaded, 16)
            nc.scalar.activation(SC[:, :, :], X0[:, :, :], ACT.Square).then_inc(squares_ready, 1)
            root(RS)
            with repeat(act, 2, (ring, BANKS)):
                for s in range(BANKS):
                    ring.wait_full()
                    nc.scalar.activation(SG[:, s, :], ring.bank()[:, S:2 * S], ACT.Sigmoid).then_inc(gate_half, 1)
                    ring.n += 1
            act.wait_ge(pads_ready, 1)
            for s in range(4):
                evacuate(ACT.Copy, PADZ[:, 2 * s:2 * s + 2, ZPAD:ZPAD + S])
            for s in range(4):
                evacuate(ACT.Gelu_apprx_tanh, U[:, 2 * s:2 * s + 2, :])
            for c in range(2):
                for tt in range(TT):
                    evacuate_tm(ACT.Gelu_apprx_tanh, VT[:, tt, c * 512:(c + 1) * 512])
            for s in range(4):
                evacuate(ACT.Sigmoid, GATES[:, 2 * s:2 * s + 2, :])
            square_halves(CV)
            root(RS)
            root(RT, TT)
            with repeat(act, 2, (ring, BANKS)) as i:
                for s in range(BANKS):
                    evacuate(ACT.Sigmoid, GATES[:, bass.ds(8 + 2 * s + i * 8, 2), :])
            for s in range(4):
                ring.wait_full()
                act.wait_ge(cols_loaded, 16)
                nc.scalar.activation(POOLMIX[:, 2 * s, :], ring.bank()[:, 0:S], ACT.Copy, scale=col("s_pool", 2 * s))
                ring.release(nc.scalar.activation(POOLMIX[:, 2 * s + 1, :], ring.bank()[:, S:2 * S], ACT.Copy,
                                                  scale=col("s_pool", 2 * s + 1)))
            gain_bias(CV, CV, "g_conv_ln", "b_conv_ln", ACT.Silu)
            ring.n += 12

            def squares_by_pair(src):
                for s in range(4):
                    square(SC[:, 2 * s:2 * s + 2, :], src[:, 2 * s:2 * s + 2, :])

            def squares_of_copies():
                for s in range(4):
                    ring.wait_stored(ring.n)
                    ring.n += 1
                    nc.scalar.activation(SC[:, 2 * s:2 * s + 2, :], MO[:, 2 * s:2 * s + 2, :], ACT.Square)\
                      .then_inc(squares_ready, 1)

            squares_of_copies()
            root(RS)
            squares_by_pair(X0)
            root(RS)
            with repeat(act, 5, (ring, BANKS)):
                for s in range(BANKS):
                    ring.wait_full()
                    nc.scalar.activation(SG[:, s, :], ring.bank()[:, 0:S], ACT.Silu).then_inc(gate_half, 1)
                    ring.n += 1
            for s in range(2):
                ring.wait_full()
                nc.scalar.activation(SG[:, s, :], ring.bank()[:, 0:S], ACT.Silu).then_inc(gate_half, 1)
                ring.n += 1
            squares_of_copies()
            root(RS)
            for s in range(4):
                evacuate(ACT.Copy, PL[:, 2 * s:2 * s + 2, :])
            for s in range(4):
                ring.wait_full()
                if s >= 2:
                    act.wait_ge(ple_gated, s - 1)
                ring.release(nc.scalar.activation(SG[:, 2 * (s % 2):2 * (s % 2) + 2, :], halves(ring.bank()), ACT.Sigmoid))
            act.wait_ge(ple_gated, 4)
            act.dma_start(POSI[:, 0, :], positions.partition_broadcast(P)).then_inc(pos_loaded, 16)
            act.dma_start(DC[:, 0, :], decay.partition_broadcast(P)).then_inc(pos_loaded, 16)
            act.wait_ge(pos_loaded, 32)
            link(nc.scalar.activation(DC[:, 1, :], DC[:, 0, :], ACT.Exp))
            link(nc.scalar.activation(DC[:, 2, :], DC[:, 1, :], ACT.Identity, scale=-1.0, bias=1.0))
            nc.scalar.activation(DC[:, 3, :], DC[:, 2, :], ACT.Ln).then_inc(freq_act, 1)
            for e in range(RET_HEADS):
                act.wait_ge(freq_dve, e + 1)
                nc.scalar.activation(DEC[:, 2 * e:2 * e + 2, :], DEC[:, 2 * e:2 * e + 2, :], ACT.Exp).then_inc(freq_act, 1)
            for f in range(2):
                act.wait_ge(freq_dve, RET_HEADS + f + 1)
                nc.scalar.activation(SIN[:, f, :], SIN[:, f, :], ACT.Sin)
                nc.scalar.activation(COS[:, f, :], COS[:, f, :], ACT.Sin).then_inc(freq_act, 1)
            ring.n += 8
            with repeat(act, 2, (ring, BANKS)) as i:
                for c in range(2):
                    for tt in range(TT):
                        evacuate_tm(ACT.Copy, V[:, tt, bass.ds(c * 512 + i * 1024, 512)])
            with repeat(act, 2, (ring, BANKS)) as i:
                for s in range(BANKS):
                    evacuate(ACT.Silu, GS[:, bass.ds(2 * s + i * 8, 2), :])
            def gain_heads(e):
                for c in (2 * e, 2 * e + 1):
                    ring.wait_full()
                    nc.scalar.activation(YG[:, 2 * c, :], ring.bank()[:, 0:S], ACT.Identity,
                                         bias=col("gn_b", 2 * c), scale=col("gn_g", 2 * c))
                    ring.release(nc.scalar.activation(YG[:, 2 * c + 1, :], ring.bank()[:, S:2 * S], ACT.Identity,
                                                      bias=col("gn_b", 2 * c + 1), scale=col("gn_g", 2 * c + 1)))

            root(RT, TT)
            root(RT, TT)
            gain_heads(0)
            root(RT, TT)
            gain_heads(1)
            root(RT, TT)
            gain_heads(2)
            gain_heads(3)
            ring.n += 4

            def peer(layer):
                square_halves(X0)
                root(RS)
                gain_bias(X0, X0, f"ln_g{layer}", f"ln_b{layer}")
                for u in range(ring.n - 4, ring.n):
                    ring.wait_stored(u)
                act.dma_start(KEYS, keys[layer]).then_inc(keys_loaded, 16)
                if layer:
                    act.wait_ge(tokens_normed, TT)
                act.dma_start(RO[:, 0:2, :], rows[3 + 2 * layer:5 + 2 * layer].partition_broadcast(P)).then_inc(rows_loaded, 16)

                def store_queries(head):
                    evacuate(ACT.Copy, QT[:, 2 * head:2 * head + 2, :])

                def store_scores(head):
                    ring.wait_full()
                    ring.release(nc.scalar.activation(
                        SCO[:, :, :].rearrange("p (t u) n -> p t u n", t=TT)[:, :, 2 * head:2 * head + 2, :],
                        ring.bank()[:, :].rearrange("p (t u n) -> p t u n", t=TT, u=2), ACT.Copy))
                    ring.wait_stored(ring.n - 1)
                    act.sem_inc(head_scored, 2 if head == HEADS - 1 else 1)

                store_queries(0)
                for tt in range(TT):
                    for half in range(2):
                        evacuate_tm(ACT.Copy, HTM[:, tt, half * 512:(half + 1) * 512])
                store_scores(0)
                store_queries(1)
                units0, b0 = layer * TT * HEADS, layer * TT * HEADS * GROUPS

                def exps(par, u, i):
                    act.wait_ge(top_ready, u if i is None else u + i * 2)
                    nc.scalar.activation(EX[:, par, :], T16[:, :], ACT.Exp, bias=NM[:, 0:1],
                                         accum_out=ES[:, par:par + 1]).then_inc(exp_ready, 1)

                def group(q, b, i):
                    act.wait_ge(dots_ready, b + 1 + i * 2 * GROUPS)
                    nc.scalar.activation(GL[:, q % 2, :], HD[:, q % 2, :], ACT.Gelu).then_inc(gelu_ready, 1)
                    act.wait_ge(group_free, PARTS * layer + b + 1 + i * 2 * GROUPS)
                    act.wait_ge(weights_ready, b + 1 + i * 2 * GROUPS)
                    for s in range(GROUP):
                        last = nc.scalar.activation(DG[:, (q % PARTS) * GROUP + s, :], IDENT[:, :], ACT.Copy,
                                                    scale=WT[:, q % 2, s:s + 1])
                    last.then_inc(diag_ready, 1)

                exps(0, units0 + 1, None)
                for head in range(2, AHEAD):
                    store_queries(head)
                    store_scores(head - 1)
                for q in range(2 * GROUPS):
                    group(q, b0 + q, 0)
                    if q % GROUPS == 0:
                        exps(1 - q // GROUPS, units0 + q // GROUPS + 2, None)
                    head = q // 2 - 1 + AHEAD
                    if q and q % 2 == 0 and head < HEADS:
                        store_queries(head)
                        store_scores(head - 1)
                    if q % 2 and head == HEADS - 1:
                        store_scores(head)
                for tt in range(TT):
                    first = 2 if tt == 0 else 0
                    with act.Fori(0, HEADS // 2 - 1) as i:
                        for q in range(2 * GROUPS):
                            group(q, b0 + (tt * HEADS + first) * GROUPS + q, i)
                            if q % GROUPS == 0:
                                exps(1 - q // GROUPS, units0 + tt * HEADS + first + q // GROUPS + 2, i)
                for q in range(2 * GROUPS):
                    group(q, b0 + (TT * HEADS - 2) * GROUPS + q, 0)
                    if q == 0:
                        exps(1, units0 + TT * HEADS, None)
                    if q == GROUPS:
                        root(RT)
                root(RT)

            peer(0)
            for s in range(4):
                evacuate(ACT.Copy, X1[:, 2 * s:2 * s + 2, :])
            for s in range(3):
                evacuate(ACT.Copy, CC[:, 2 * s:2 * s + 2, :])
            ring.wait_full()
            ring.release(nc.scalar.activation(CC[:, 6, :], ring.bank()[:, 0:S], ACT.Copy))
            for u in range(ring.n - 4, ring.n):
                ring.wait_stored(u)
            nc.scalar.activation(SC[:, 0:3, :], CC[:, 0:3, :], ACT.Square).then_inc(squares_ready, 1)
            nc.scalar.activation(SC[:, 3:5, :], CC[:, 3:5, :], ACT.Square).then_inc(squares_ready, 1)
            root(RS, 2)
            for s in range(6):
                evacuate(ACT.Copy, QN[:, 2 * s:2 * s + 2, :])
            for s in range(4):
                evacuate(ACT.Copy, KN[:, 2 * s:2 * s + 2, :])
            for c in range(2):
                for tt in range(TT):
                    evacuate_tm(ACT.Copy, VM[:, tt, c * 512:(c + 1) * 512])

            def probs_exp(e):
                act.wait_ge(mla_max, e + 1)
                for qt in range(TT):
                    nc.scalar.activation(PS[:, 2 * e + qt, :], AUX[e % 2][:, qt * S:(qt + 1) * S], ACT.Exp,
                                         bias=MX[:, e, qt:qt + 1], scale=MLA_SCALE,
                                         accum_out=SU[:, e, qt:qt + 1]).then_inc(mla_exp, 1)

            for e in range(MLA_HEADS + 2):
                if e < MLA_HEADS:
                    probs_exp(e)
                if 0 <= e - 1 < MLA_HEADS:
                    act.wait_ge(mla_turned, e)
                    nc.scalar.activation(PTT[:, 2 * e - 2:2 * e, :], halves(AUX[2 + (e - 1) % 2]), ACT.Copy)\
                      .then_inc(mla_probs_cm, 1)
                if e >= 2 and (e - 2) % 2:
                    evacuate(ACT.Copy, OM[:, e - 3:e - 1, :])
            ring.n += 4
            peer(1)

        @block.vector
        def _(dve):
            chain = Chain(dve, dve_chain, waits_passed)
            link, link_alone = chain.link, chain.link_alone
            ring = Turns(dve, acc_full, acc_free, ACC)
            v = nc.vector
            n = dict(sums=0, roots=0)

            def wide(a, k=KT):
                return a[:, None, :].broadcast_to([P, k, S])

            def sums_done():
                n["sums"] += 1
                dve.wait_ge(sums_ready, n["sums"])

            def rooted(dst, ins):
                n["roots"] += 1
                ins.then_inc(var_ready, 1)
                dve.wait_ge(root_ready, n["roots"])
                link(v.reciprocal(dst, dst))

            def rstd(half, width, eps):
                sums_done()
                rooted(RS[:, :], v.tensor_scalar(RS[:, :], AUX[3 - half][:, 0:S], 1.0 / width, eps,
                                                 ALU.mult, ALU.add))

            def rms_apply(dst, src, g, k0, k1, g0=0):
                for k in range(k0, k1):
                    last = v.scalar_tensor_tensor(dst[:, k, :], src[:, k, :], col(g, k - g0), RS[:, :], ALU.mult, ALU.mult)
                return last

            def centre(x):
                sums_done()
                link(v.tensor_scalar(MU[:, :], AUX[3][:, 0:S], 1.0 / D, None, ALU.mult))
                for k in (0, KT // 2):
                    half = x[:, k:k + KT // 2, :]
                    v.tensor_tensor(half, half, wide(MU, KT // 2), ALU.subtract).then_inc(centred, 1)

            def layer_scale(x, eps):
                rstd(1, D, eps)
                for k in (0, KT // 2):
                    half = x[:, k:k + KT // 2, :]
                    v.tensor_tensor(half, half, wide(RS, KT // 2), ALU.mult).then_inc(scaled, 1)

            dve.wait_ge(cols_loaded, 16)
            dve.wait_ge(x_loaded, 16)
            rstd(0, D, EPS)
            for k in (0, KT // 2):
                rms_apply(X1, X0, "g_mix_pre", k, k + KT // 2).then_inc(input_ready, 1)

            def taps(j):
                for k in range(CONV):
                    for c in range(2):
                        at = PADH[:, j + c, k:k + S]
                        w = CO[:, bass.ds((j + c) * CONV + (COL["w_dw"] + k), 1)]
                        if k == 0:
                            chain.step(v.tensor_scalar(CV[:, j + c, :], at, w, CO[:, bass.ds(j + (COL["b_dw"] + c), 1)],
                                                       ALU.mult, ALU.add))
                        else:
                            chain.wait_back(1)
                            chain.step(v.scalar_tensor_tensor(CV[:, j + c, :], at, w, CV[:, j + c, :], ALU.mult, ALU.add))
                chain.wait_back(0)

            dve.wait_ge(pads_ready, 1)
            with repeat(dve, 2, (ring, BANKS), (chain, 2 * CONV)) as i:
                for s in range(BANKS):
                    ring.wait_full()
                    dve.wait_ge(gate_half, s + 1 + i * BANKS)
                    ins = v.tensor_tensor(PADH[:, s + i * BANKS, PAD:PAD + S], ring.bank()[:, 0:S], SG[:, s, :], ALU.mult)
                    ring.release(ins)
                for u in range(ring.n - BANKS, ring.n):
                    ring.wait_stored(u)
                taps(i * 2)
            with repeat(dve, 2, (chain, 2 * CONV)) as i:
                taps(i * 2 + 4)
            dve.sem_inc(input_ready, 1)
            centre(CV)
            layer_scale(CV, EPS)
            ring.n += 8
            dve.wait_ge(rows_loaded, 16)
            for u in range(ring.n, ring.n + 4):
                ring.wait_stored(u)
            ring.n += 4
            for tt in range(TT):
                for c in range(2):
                    last = v.bn_stats(BN[:, c, :], VT[:, tt, c * 512:(c + 1) * 512])
                    if c:
                        link(last)
                link(v.bn_aggr(MV[:, :], BN[:, :, :]))
                rooted(RT[:, :], v.tensor_scalar(RT[:, :], MV[:, 1:2], EPS, None, ALU.add))
                link(v.tensor_scalar(VT[:, tt, :], VT[:, tt, :], MV[:, 0:1], RT[:, 0:1], ALU.subtract, ALU.mult))
                link(v.tensor_tensor(VT[:, tt, :], VT[:, tt, :], RO[:, 0, :], ALU.mult))
                last = v.tensor_tensor(VT[:, tt, :], VT[:, tt, :], RO[:, 1, :], ALU.add)
                link(last) if tt == 0 else last.then_inc(input_ready, 1)
            ring.n += 12 + 4
            for s in range(4):
                dve.wait_ge(mix_ready, s + 1)
                o = AIN[:, 2 * s:2 * s + 2, :]
                bias = RO[:, 2, 2 * s * P:(2 * s + 2) * P].rearrange("p (h i) -> p h i", i=P)[:, :, None, :]\
                    .broadcast_to([P, 2, TT, P])
                link(v.tensor_tensor(o.rearrange("p h (b i) -> p h b i", b=TT),
                                     AUX[s][:, :].rearrange("p (h b i) -> p h b i", h=2, b=TT), bias, ALU.add))
                last = v.tensor_tensor(o, o, U[:, 2 * s:2 * s + 2, :], ALU.mult)
            last.then_inc(input_ready, 1)
            for step, g in enumerate((1, 2, 0)):
                for s in range(4):
                    gate = GATES[:, KT * g + 2 * s:KT * g + 2 * s + 2, :]
                    dst = MERGED[:, 2 * s:2 * s + 2, :]
                    ring.wait_full()
                    if step == 0:
                        ring.release(v.tensor_tensor(dst, halves(ring.bank()), gate, ALU.mult))
                        continue
                    tmp = SG[:, 2 * (s % 2):2 * (s % 2) + 2, :]
                    ring.release(v.tensor_tensor(tmp, halves(ring.bank()), gate, ALU.mult))
                    ring.wait_stored(ring.n - 1)
                    last = v.tensor_tensor(dst, dst, tmp, ALU.add)
                    if step == 2 and s == 3:
                        last.then_inc(input_ready, 1)
                    else:
                        link(last)

            def copy_out(dst):
                for s in range(4):
                    ring.wait_full()
                    ring.release(v.tensor_copy(dst[:, 2 * s:2 * s + 2, :], halves(ring.bank())))

            def add_normed(g, signal):
                rstd(0, D, EPS)
                for s in range(4):
                    link(rms_apply(MO, MO, g, 2 * s, 2 * s + 2))
                    last = v.tensor_tensor(X0[:, 2 * s:2 * s + 2, :], X0[:, 2 * s:2 * s + 2, :],
                                           MO[:, 2 * s:2 * s + 2, :], ALU.add)
                    if signal is not None:
                        last.then_inc(signal, 1)
                    else:
                        link(last)

            copy_out(MO)
            add_normed("g_mix_post", centred)
            rstd(0, D, EPS)
            for k in (0, KT // 2):
                rms_apply(X1, X0, "g_ffn_pre", k, k + KT // 2).then_inc(input_ready, 1)
            gh = 8
            with repeat(dve, 5, (ring, BANKS)) as i:
                for s in range(BANKS):
                    ring.wait_full()
                    dve.wait_ge(gate_half, gh + s + 1 + i * BANKS)
                    ring.release(v.tensor_tensor(F[:, s + i * BANKS, :], ring.bank()[:, S:2 * S], SG[:, s, :], ALU.mult))
            for s in range(2):
                ring.wait_full()
                dve.wait_ge(gate_half, gh + 20 + s + 1)
                ring.release(v.tensor_tensor(F[:, 20 + s, :], ring.bank()[:, S:2 * S], SG[:, s, :], ALU.mult))
            copy_out(MO)
            add_normed("g_ffn_post", None)
            dve.sem_inc(input_ready, 1)
            ple0 = ring.n
            ring.n += 4
            for s in range(4):
                ring.wait_stored(ple0 + s)
                ring.wait_stored(ring.n)
                ring.n += 1
                sg = SG[:, 2 * (s % 2):2 * (s % 2) + 2, :]
                t = PL[:, 2 * s:2 * s + 2, :]
                link(v.tensor_tensor(t, t, sg, ALU.mult))
                link(v.tensor_tensor(X1[:, 2 * s:2 * s + 2, :], X0[:, 2 * s:2 * s + 2, :], t, ALU.add))
                dve.sem_inc(ple_gated, 1)
            dve.sem_inc(input_ready, 1)
            dve.wait_ge(iota_ready, 2)
            link(v.tensor_copy(DNEG, DIFI))
            link(v.tensor_scalar(DIFF, DNEG, 0.0, None, ALU.max))
            link(v.tensor_scalar(DNEG, DNEG, 0.0, -1.0, ALU.min, ALU.mult))
            dve.wait_ge(freq_act, 1)
            link(v.tensor_scalar(DC[:, 2, :], DC[:, 2, :], -1.0, 1.0, ALU.mult, ALU.add))
            link(v.tensor_scalar(DC[:, 0, :], DC[:, 2, :], 1e-30, None, ALU.max))
            link(v.reciprocal(DC[:, 0, :], DC[:, 0, :]))
            link(v.tensor_tensor(DC[:, 3, :], DC[:, 3, :], DC[:, 0, :], ALU.mult))
            link(v.tensor_tensor(DC[:, 3, :], DC[:, 3, :], DC[:, 1, :], ALU.mult))
            link(v.tensor_scalar(DC[:, 4, :], DC[:, 2, :], 0.0, None, ALU.is_equal))
            link(v.tensor_tensor(DC[:, 4, :], DC[:, 4, :], DC[:, 1, :], ALU.mult))
            link(v.tensor_tensor(DC[:, 3, :], DC[:, 3, :], DC[:, 4, :], ALU.subtract))
            for e in range(RET_HEADS):
                dst = DEC[:, 2 * e:2 * e + 2, :]
                link(v.tensor_scalar(dst, DIFF, DC[:, 3, e:e + 1], None, ALU.mult))
                v.scalar_tensor_tensor(dst, DNEG, DC[:, 3, RET_HEADS + e:RET_HEADS + e + 1], dst, ALU.mult, ALU.add)\
                 .then_inc(freq_dve, 1)
            dve.wait_ge(pos_loaded, 32)
            link(v.tensor_copy(POSF, POSI))
            for f, name in enumerate(("freq_ret", "freq_mla")):
                link(v.tensor_scalar(ANG, POSF, col(name), None, ALU.mult))
                link(v.tensor_scalar(TURN, ANG, 1.0 / TWO_PI, ROUND, ALU.mult, ALU.add))
                link(v.tensor_scalar(TURN, TURN, ROUND, None, ALU.subtract))
                for part in (PI_A, PI_B, PI_C):
                    link(v.scalar_tensor_tensor(ANG, TURN, -part, ANG, ALU.mult, ALU.add))
                link(v.tensor_scalar(SIN[:, f:f + 1, :], ANG, 3.1415925, -3.1415925, ALU.min, ALU.max))
                link(v.tensor_scalar(ANG, SIN[:, f:f + 1, :], -1.0, None, ALU.mult))
                link(v.tensor_tensor(ANG, ANG, SIN[:, f:f + 1, :], ALU.max))
                link(v.tensor_scalar(COS[:, f:f + 1, :], ANG, -1.0, math.pi / 2, ALU.mult, ALU.add))
                dve.sem_inc(freq_dve, 1)
            dve.wait_ge(freq_act, 1 + RET_HEADS + 1)

            def rotate(src, f):
                cos, sin = (a[:, f, :][:, None, :].broadcast_to([P, 2, S]) for a in (COS, SIN))
                v.tensor_tensor(RA, src, cos, ALU.mult)
                return v.tensor_tensor(RB, src, sin, ALU.mult)

            with repeat(dve, 2, (ring, BANKS), (chain, BANKS)) as i:
                for s in range(BANKS):
                    ring.wait_full()
                    ins = rotate(halves(ring.bank()), 0)
                    free, count = acc_free[ring.n % BANKS], ring.n // BANKS + 1
                    ring.release(ins)
                    dve.wait_ge(free, count + i)
                    v.tensor_tensor(QK[:, bass.ds(2 * s + i * 8, 1), :], RA[:, 0:1, :], RB[:, 1:2, :], ALU.subtract)
                    link(v.tensor_tensor(QK[:, bass.ds(2 * s + 1 + i * 8, 1), :], RB[:, 0:1, :], RA[:, 1:2, :], ALU.add))
            dve.sem_inc(input_ready, 1)
            ring.n += 8
            for e in range(RET_HEADS):
                dve.wait_ge(scores_ready, e + 1)
                dve.wait_ge(freq_act, 2 + e)
                v.scalar_tensor_tensor(PR[:, 2 * e:2 * e + 2, :], halves(AUX[e]), RET_DK ** -0.5,
                                       DEC[:, 2 * e:2 * e + 2, :], ALU.mult, ALU.mult).then_inc(probs_ready, 1)
            ring.n += 8
            g_uses = ring.n

            def group_norm(e):
                for nt in range(TT):
                    bank = AUX[2 * (e % 2) + nt]
                    dve.wait_ge(y_ready, 2 * e + nt + 1)
                    link(v.bn_stats(BN[:, 0, :], bank[:, :]))
                    if e or nt:
                        dve.wait_ge(yn_ready, 2 * e + nt)
                    link(v.bn_aggr(MV[:, :], BN[:, 0, :]))
                    rooted(RT[:, :], v.tensor_scalar(RT[:, :], MV[:, 1:2], LN_EPS, None, ALU.add))
                    v.tensor_scalar(YN[:, 2 * e + nt, :], bank[:, :], MV[:, 0:1], RT[:, 0:1], ALU.subtract,
                                    ALU.mult).then_inc(yn_ready, 1)

            def gate_heads(e):
                for c in (2 * e, 2 * e + 1):
                    ring.wait_stored(ring.n)
                    ring.n += 1
                    last = v.tensor_tensor(YG[:, 2 * c:2 * c + 2, :], YG[:, 2 * c:2 * c + 2, :],
                                           GS[:, 2 * c:2 * c + 2, :], ALU.mult)
                return last

            for u in range(g_uses - 4, g_uses):
                ring.wait_stored(u)
            group_norm(0)
            group_norm(1)
            gate_heads(0)
            group_norm(2)
            gate_heads(1)
            group_norm(3)
            gate_heads(2)
            gate_heads(3).then_inc(input_ready, 1)

            def add_residual(h):
                for s in range(4):
                    ring.wait_full()
                    ring.release(v.scalar_tensor_tensor(X0[:, 2 * s:2 * s + 2, :], h[:, 2 * s:2 * s + 2, :], ALPHA,
                                                        halves(ring.bank()), ALU.mult, ALU.add))

            add_residual(X1)

            def peer(layer):
                centre(X0[:, :, :])
                layer_scale(X0[:, :, :], LN_EPS)
                token_uses = ring.n + 1
                ring.n += 2 * TT + 2 * HEADS
                dve.wait_ge(iota_ready, 1)
                scored = (HEADS + 1) * layer
                dve.wait_ge(head_scored, scored + 1)
                units0, b0 = layer * TT * HEADS, layer * TT * HEADS * GROUPS

                def topk(par, unit, i):
                    at = SCO[:, 2 * unit:2 * unit + 2, :] if i is None else SCO[:, bass.ds(2 * unit + i * 4, 2), :]
                    link_alone(v.tensor_copy(SK, at))
                    for c in range(2):
                        link_alone(v.max(M16[:, c, 0:8], SK[:, c, :]))
                        v.max_index(I16[:, c, 0:8], M16[:, c, 0:8], SK[:, c, :])
                        link_alone(v.match_replace(SL[:, c, :], M16[:, c, 0:8], SK[:, c, :], LOWEST))
                        link_alone(v.max(M16[:, c, 8:16], SL[:, c, :]))
                        link_alone(v.max_index(I16[:, c, 8:16], M16[:, c, 8:16], SL[:, c, :]))
                    link_alone(v.tensor_tensor(CA[:, 0, :].rearrange("p (a b) -> p a b", b=TOPK),
                                               M16[:, 0, :][:, :, None].broadcast_to([P, TOPK, TOPK]),
                                               M16[:, 1, :][:, None, :].broadcast_to([P, TOPK, TOPK]), ALU.add))
                    link_alone(v.max(T16[:, 0:8], CA[:, 0, :]))
                    v.max_index(P16[:, 0:8], T16[:, 0:8], CA[:, 0, :])
                    link_alone(v.match_replace(CB[:, 0, :], T16[:, 0:8], CA[:, 0, :], LOWEST))
                    link_alone(v.max(T16[:, 8:16], CB[:, 0, :]))
                    v.max_index(P16[:, 8:16], T16[:, 8:16], CB[:, 0, :])
                    v.tensor_copy(IF16[:, :, :], I16[:, :, :])
                    link(v.tensor_scalar(NM[:, :], T16[:, 0:1], -1.0, None, ALU.mult))
                    dve.sem_inc(top_ready, 1)
                    v.tensor_scalar(AB[:, 0, :], P16[:, :], 4, None, ALU.logical_shift_right)
                    link(v.tensor_scalar(AB[:, 1, :], P16[:, :], 15, None, ALU.bitwise_and))
                    link(v.tensor_copy(ABF[:, :, :], AB[:, :, :]))
                    oh = OH[:, :, :].rearrange("p c (k a) -> p c k a", a=TOPK)
                    link(v.tensor_tensor(oh, ABF[:, :, :][:, :, :, None].broadcast_to([P, 2, TOPK, TOPK]),
                                         IOTA16[:, None, None, :].broadcast_to([P, 2, TOPK, TOPK]), ALU.is_equal))
                    link(v.tensor_tensor(oh, oh, IF16[:, :, :][:, :, None, :].broadcast_to([P, 2, TOPK, TOPK]), ALU.mult))
                    link(v.tensor_reduce(EI[:, :, :], oh, AX.X, ALU.add))
                    v.scalar_tensor_tensor(EIDX[:, par, :], EI[:, 0, :], float(NKEYS), EI[:, 1, :], ALU.mult,
                                           ALU.add).then_inc(idx_ready, 1)

                LINKS_TOPK = 1 + 2 * 4 + 1 + 3 + 1 + 5

                def gates(par, unit, i):
                    dve.wait_ge(exp_ready, unit if i is None else unit + i * 2)
                    link(v.reciprocal(ES[:, par:par + 1], ES[:, par:par + 1]))
                    link(v.tensor_scalar(GT[:, par, :], EX[:, par, :], ES[:, par:par + 1], None, ALU.mult))

                def group(tt, q, b, i):
                    for s in range(GROUP):
                        slot = (q % PARTS) * GROUP + s
                        dve.wait_ge(gathered[slot], 16 * (b // PARTS + 1) + i * 16 * (2 * GROUPS // PARTS))
                        last = v.scalar_tensor_tensor(G[:, slot, 0:D], G[:, slot, 0:D], 1.0, HTM[:, tt, :], ALU.mult,
                                                      ALU.mult, accum_out=HD[:, q % 2, s:s + 1])
                    last.then_inc(dots_ready, 1)
                    dve.wait_ge(gelu_ready, b + 1 + i * 2 * GROUPS)
                    k = (q % GROUPS) * GROUP
                    v.tensor_tensor(WT[:, q % 2, :], GL[:, q % 2, :], GT[:, q // GROUPS, k:k + GROUP],
                                    ALU.mult).then_inc(weights_ready, 1)

                def output_norm(tt):
                    dve.wait_ge(experts_summed, TT * layer + tt + 1)
                    for c in range(2):
                        last = v.bn_stats(BN[:, c, :], AUX[2 * tt + c][:, :])
                    link(last)
                    link(v.bn_aggr(MV[:, :], BN[:, :, :]))
                    rooted(RT[:, :], v.tensor_scalar(RT[:, :], MV[:, 1:2], LN_EPS, None, ALU.add))
                    for c in range(2):
                        last = v.tensor_scalar(HTM[:, tt, c * 512:(c + 1) * 512], AUX[2 * tt + c][:, :], MV[:, 0:1],
                                               RT[:, 0:1], ALU.subtract, ALU.mult)
                    link(last)
                    link(v.tensor_tensor(HTM[:, tt, :], HTM[:, tt, :], RO[:, 0, :], ALU.mult))
                    v.tensor_tensor(HTM[:, tt, :], HTM[:, tt, :], RO[:, 1, :], ALU.add).then_inc(tokens_normed, 1)

                topk(0, 0, None)
                gates(0, units0 + 1, None)
                for u in range(token_uses, token_uses + 2 * TT):
                    ring.wait_stored(u)
                dve.wait_ge(rows_loaded, 32 + 16 * layer)
                for tt in range(TT):
                    loops = HEADS // 2 - tt
                    with repeat(dve, loops, (chain, 2 * (LINKS_TOPK + 2))) as i:
                        for q in range(2 * GROUPS):
                            group(tt, q, b0 + tt * HEADS * GROUPS + q, i)
                            if q % GROUPS == 0:
                                unit = tt * HEADS + q // GROUPS + 1
                                if tt == 0:
                                    dve.wait_ge(head_scored, scored + unit + 1 + i * 2)
                                    dve.sem_inc(waits_passed, 1)
                                topk(1 - q // GROUPS, unit, i)
                                gates(1 - q // GROUPS, units0 + unit + 1, i)
                for q in range(2 * GROUPS):
                    group(1, q, b0 + (TT * HEADS - 2) * GROUPS + q, 0)
                    if q == 0:
                        topk(1, TT * HEADS - 1, None)
                        gates(1, units0 + TT * HEADS, None)
                    if q == GROUPS:
                        output_norm(0)
                output_norm(1)

            peer(0)
            ring.n += 4
            c_uses = ring.n
            ring.n += 4
            for u in range(c_uses, ring.n):
                ring.wait_stored(u)
            rstd(0, 384, LN_EPS)
            link(rms_apply(CN, CC, "q_norm", 0, 3))
            rstd(1, 256, LN_EPS)
            link(rms_apply(CN, CC, "kv_norm", 3, 5, 3))
            dve.sem_inc(input_ready, 1)
            dve.wait_ge(freq_act, 1 + RET_HEADS + 2)

            def rotate_mla(dst, k, src):
                link(rotate(src, 1))
                v.tensor_tensor(dst[:, k[0], :], RA[:, 0, :], RB[:, 1, :], ALU.subtract)
                link(v.tensor_tensor(dst[:, k[1], :], RB[:, 0, :], RA[:, 1, :], ALU.add))

            rotate_mla(KR, (0, 1), CC[:, 5:7, :])
            for r in range(2):
                for q in range(4):
                    v.tensor_scalar(KRM[:, 4 * r + q, :], KR[:, r, :], col("quarter", q), None, ALU.mult)
            uq = ring.n
            ring.n += 6 + 4 + 4
            ring.wait_stored(uq + 4)
            ring.wait_stored(uq + 5)
            for half in range(2):
                rotate_mla(QR, (half, 2 + half), QN[:, 8 + half:11 + half:2, :])
            dve.sem_inc(input_ready, 1)

            def probs_max(e):
                dve.wait_ge(mla_scored, e + 1)
                link(v.tensor_reduce(MX[:, e, :], halves(AUX[e % 2]), AX.X, ALU.max))
                v.tensor_scalar(MX[:, e, :], MX[:, e, :], -MLA_SCALE, None, ALU.mult).then_inc(mla_max, 1)

            def probs_norm(e):
                dve.wait_ge(mla_exp, 2 * (e + 1))
                link(v.reciprocal(SU[:, e, :], SU[:, e, :]))
                for qt in range(TT):
                    last = v.tensor_scalar(PS[:, 2 * e + qt, :], PS[:, 2 * e + qt, :], SU[:, e, qt:qt + 1], None, ALU.mult)
                last.then_inc(mla_prob, 1)

            probs_max(0)
            for e in range(MLA_HEADS):
                if e + 1 < MLA_HEADS:
                    probs_max(e + 1)
                probs_norm(e)
            ring.n += 4
            add_residual(X1)
            peer(1)


def _tiles(w, order):
    import numpy as np
    return [w[k * P:(k + 1) * P, n * P:(n + 1) * P] for k, n in order]


def _cm(n_tiles, kt):
    return [(k, n) for n in n_tiles for k in range(kt)]


def _tm(n_tiles, kt):
    return [(k, n) for c in range(0, len(n_tiles), 4) for k in range(kt) for n in n_tiles[c:c + 4]]


def _layout(inputs):
    import numpy as np
    f = lambda name: np.asarray(inputs[name])
    w_in = f("w_in")[0]
    t = []
    seq = range
    t += _tiles(w_in, _cm([n for j in seq(8) for n in (16 + j, 24 + j)], 8))
    t += _tiles(w_in, _cm(seq(32, 40), 8))
    t += _tiles(w_in, _cm(seq(0, 8), 8))
    t += _tiles(w_in, _tm(list(seq(8, 16)), 8))
    t += _tiles(w_in, _cm(seq(40, 64), 8))
    for g in range(4):
        t += _tiles(f("w_pool")[0, g], _cm(seq(2), 2))
    for name in ("w_conv_out", "w_pool_out", "w_sgu_out", "w_out"):
        t += _tiles(f(name)[0], _cm(seq(8), 8))
    t += _tiles(f("w_ffn_in")[0], _cm([n for j in seq(FT) for n in (j, FT + j)], 8))
    t += _tiles(f("w_ffn_out")[0], _cm(seq(8), FT))
    t += _tiles(f("w_ple")[0], _cm(seq(8), 2))
    t += _tiles(f("w_ple_gate")[0], _cm(seq(8), 8))
    ret = f("ret_w_in_2")[0]
    t += _tiles(ret, _cm(seq(0, 16), 8))
    t += _tiles(ret, _tm(list(seq(16, 32)), 8))
    t += _tiles(ret, _cm(seq(32, 48), 8))
    t += _tiles(f("ret_w_out_2")[0], _cm(seq(8), 16))

    t += _tiles(f("peer_w_q_2")[0], _cm(seq(16), 8))
    m = f("mla_w_in_2")[0]
    r1, r2 = m[:, 640:672], m[:, 672:704]
    m = np.concatenate([m[:, :640]] + [r1] * 4 + [r2] * 4, axis=1)
    t += _tiles(m, _cm(seq(7), 8))
    uq = f("mla_w_uq_2")[0].reshape(384, MLA_HEADS, 192)
    uq = np.concatenate([uq[:, :, :128].reshape(384, -1), uq[:, :, 128:160].reshape(384, -1),
                         uq[:, :, 160:].reshape(384, -1)], axis=1)
    t += _tiles(uq, _cm(seq(12), 3))
    t += [np.zeros((P, P), np.float32)] * 4
    ukv = f("mla_w_ukv_2")[0]
    t += _tiles(ukv, _cm([2 * e for e in seq(8)], 2))
    t += _tiles(ukv, _tm([2 * e + 1 for e in seq(8)], 2))
    t += _tiles(f("mla_w_out_2")[0], _cm(seq(8), 8))
    t += _tiles(f("peer_w_q_2")[1], _cm(seq(16), 8))
    assert len(t) == BLOCKS * TILES, (len(t), BLOCKS * TILES)
    stream = np.empty((BLOCKS, P, TILES, P), np.float32)
    for i, a in enumerate(t):
        stream[i // TILES, :, i % TILES, :] = a

    def chan(a):
        return np.asarray(a).reshape(-1, P).T

    def freqs(d):
        return np.float32(10000.0) ** (-np.arange(0, d, 2, dtype=np.float32) / np.float32(d))

    cols = {
        "g_mix_pre": chan(f("g_mix_pre")[0]),
        "w_dw": f("w_dw")[0, :, 0, :].reshape(CONV, KT, P).transpose(2, 1, 0).reshape(P, -1),
        "b_dw": chan(f("b_dw")[0]), "g_conv_ln": chan(f("g_conv_ln")[0]), "b_conv_ln": chan(f("b_conv_ln")[0]),
        "s_pool": chan(f("s_pool")[0]), "g_mix_post": chan(f("g_mix_post")[0]),
        "g_ffn_pre": chan(f("g_ffn_pre")[0]), "g_ffn_post": chan(f("g_ffn_post")[0]),
        "gn_g": chan(f("ret_gn_g_2")[0]), "gn_b": chan(f("ret_gn_b_2")[0]),
        "q_norm": chan(f("mla_q_norm_2")[0]), "kv_norm": chan(f("mla_kv_norm_2")[0]),
        "ln_g0": chan(f("ln_mix_g_2")[0]), "ln_b0": chan(f("ln_mix_b_2")[0]),
        "ln_g1": chan(f("ln_mix_g_2")[1]), "ln_b1": chan(f("ln_mix_b_2")[1]),
        "freq_ret": freqs(RET_DK)[:, None], "freq_mla": np.tile(freqs(64), 4)[:, None],
        "quarter": (np.arange(P)[:, None] // 32 == np.arange(4)[None, :]).astype(np.float32),
    }
    cols = np.concatenate([cols[name] for name, _ in _COLS], axis=1)
    rows = np.stack([f("g_sgu_v")[0], f("b_sgu_v")[0], f("b_sgu_s")[0].reshape(-1), f("ln_ffn_g_2")[0],
                     f("ln_ffn_b_2")[0], f("ln_ffn_g_2")[1], f("ln_ffn_b_2")[1]])

    def cm(a):
        return a.T.reshape(-1, P, S).transpose(1, 0, 2)

    t1 = np.arange(1, S + 1, dtype=np.float32)
    return {
        "stream": stream,
        "keys": f("peer_sub_keys_2").reshape(2, 2 * HEADS, NKEYS, P).transpose(0, 3, 1, 2), "cols": cols, "rows": rows, "x_cm": cm(f("x")[0]), "p_cm": cm(f("p")[0, 0]),
        "sgu_wt": f("w_sgu_s")[0].transpose(2, 0, 1),
        "rcnt": np.stack([1.0 / np.minimum(t1, np.float32(w)) for w in WINDOWS]).astype(np.float32),
        "positions": f("positions_2")[0], "decay": f("ret_log1m_decay_2")[0].reshape(-1),
        "uv0": np.concatenate([f("peer_u_2")[0], f("peer_v_2")[0]], axis=1),
        "uv1": np.concatenate([f("peer_u_2")[1], f("peer_v_2")[1]], axis=1),
    }


def kernel(**inputs):
    import numpy as np
    import concourse.bacc as bacc
    from concourse.bass_utils import run_bass_kernel_spmd as run

    nc = bacc.Bacc("TRN2", target_bir_lowering=False, num_devices=1)
    arrays = {k: np.ascontiguousarray(a) for k, a in _layout(inputs).items()}
    ap = {k: nc.dram_tensor(k, a.shape, mybir.dt.from_np(a.dtype), kind="ExternalInput").ap() for k, a in arrays.items()}
    out = nc.dram_tensor("out", (1, S, D), FP32, kind="ExternalOutput").ap()
    build(nc, ap["stream"], ap["keys"], ap["cols"], ap["rows"], ap["x_cm"], ap["p_cm"], ap["sgu_wt"], ap["rcnt"],
          ap["positions"], ap["decay"], ap["uv0"], ap["uv1"], out)
    return run(nc, [arrays], core_ids=[0]).results[0]["out"]
```
